# Optimizing a Trainium2 kernel written in Bass

```python
import math
import jax, jax.numpy as jnp
from jax import lax
import numpy as np

D_MODEL = 1024
BATCH = 1
SEQ = 256
DEPTH = 2

D_PLE = 256
N_A_LAYERS = DEPTH // 2
N_B_LAYERS = DEPTH - N_A_LAYERS
N_DENSE = (DEPTH + 1) // 2
N_MOE = DEPTH // 2
EPS = 1e-6

D_RNN = D_MODEL
CONV_WIDTH = 4
LRU_BLOCKS = 16
LRU_BLOCK_W = D_RNN // LRU_BLOCKS
LRU_C = 8.0

N_HEADS = 16
N_KV_GROUPS = 2
GROUP = N_HEADS // N_KV_GROUPS
HEAD_DIM = 64
N_KV_BRANCH = 6
CMP_BLOCK = 32
CMP_STRIDE = 16
CMP_HIDDEN = 256
SLC_BLOCK = 64
N_SELECT = 8
WINDOW = 512
Q_BLOCK = 128

N_BUCKETS = 32
MAX_DISTANCE = 128

D_FF = 3072
N_EXPERTS = 8
TOP_K = 2
D_FF_EXPERT = 3584

kernel_name = 'hybrid_rglru_nsa_moe_trunk'

def rmsnorm(x, g):
    xf = x.astype(jnp.float32)
    y = xf * lax.rsqrt(jnp.mean(xf * xf, axis=-1, keepdims=True) + EPS)
    return (y * g.astype(jnp.float32)).astype(x.dtype)

def masked_softmax(logits, mask):
    l = jnp.where(mask, logits.astype(jnp.float32), -1e30)
    m = jnp.max(l, axis=-1, keepdims=True)
    e = jnp.where(mask, jnp.exp(l - m), 0.0)
    return e / jnp.maximum(jnp.sum(e, axis=-1, keepdims=True), 1e-30)

def rel_bucket(dist):
    n = jnp.maximum(dist, 0)
    max_exact = N_BUCKETS // 2
    nf = jnp.maximum(n, 1).astype(jnp.float32)
    large = max_exact + (jnp.log(nf / max_exact) / math.log(MAX_DISTANCE / max_exact) * (N_BUCKETS - max_exact)).astype(jnp.int32)
    return jnp.where(n < max_exact, n, jnp.minimum(large, N_BUCKETS - 1))

def causal_dwconv(x, w, b):
    S = x.shape[1]
    xp = jnp.pad(x, ((0, 0), (CONV_WIDTH - 1, 0), (0, 0)))
    return sum(xp[:, k:k + S] * w[k] for k in range(CONV_WIDTH)) + b

def block_diag_linear(x, w, b):
    xb = x.reshape(x.shape[:-1] + (LRU_BLOCKS, LRU_BLOCK_W))
    return jnp.einsum('bsnc,ncd->bsnd', xb, w).reshape(x.shape) + b

def rg_lru(x, w_a, b_a, w_x, b_x, lam):
    f32 = jnp.float32
    r = jax.nn.sigmoid(block_diag_linear(x, w_a, b_a)).astype(f32)
    i = jax.nn.sigmoid(block_diag_linear(x, w_x, b_x)).astype(f32)
    log_a = -LRU_C * r * jax.nn.softplus(-lam.astype(f32))
    a = jnp.exp(log_a)
    u = jnp.sqrt(-jnp.expm1(2.0 * log_a)) * (i * x.astype(f32))

    def combine(c1, c2):
        a1, b1 = c1
        a2, b2 = c2
        return a1 * a2, a2 * b1 + b2

    _, h = lax.associative_scan(combine, (a, u), axis=1)
    return h.astype(x.dtype)

def recurrent_block(xn, w_in, conv_w, conv_b, w_a, b_a, w_x, b_x, lam, w_out):
    gate, xr = jnp.split(xn @ w_in, 2, axis=-1)
    xr = causal_dwconv(xr, conv_w, conv_b)
    h = rg_lru(xr, w_a, b_a, w_x, b_x, lam)
    return (jax.nn.gelu(gate) * h) @ w_out

def swiglu(x, w_gu, w_down):
    g, u = jnp.split(x @ w_gu, 2, axis=-1)
    return (jax.nn.silu(g) * u) @ w_down

def moe_ffn(x, w_router, w_gu, w_down):
    logits = (x @ w_router).astype(jnp.float32)
    top_val, top_idx = lax.top_k(logits, TOP_K)
    top_w = jax.nn.softmax(top_val, axis=-1)
    combine = jnp.sum(jax.nn.one_hot(top_idx, N_EXPERTS, dtype=jnp.float32) * top_w[..., None], axis=-2)
    combine = combine.astype(x.dtype)
    y = jnp.zeros_like(x)
    for e in range(N_EXPERTS):
        y = y + combine[..., e:e + 1] * swiglu(x, w_gu[e], w_down[e])
    return y

def nsa_shared_kv(x, kv_norm, w_kv, cmp_pos_k, cmp_pos_v, cmp_k_w1, cmp_k_w2, cmp_v_w1, cmp_v_w2):
    B, S, _ = x.shape
    kv = (rmsnorm(x, kv_norm) @ w_kv).reshape(B, S, N_KV_BRANCH, N_KV_GROUPS, HEAD_DIM)
    k_ct, v_ct, k_slc, v_slc, k_win, v_win = [kv[:, :, j] for j in range(N_KV_BRANCH)]
    n_cmp = (S - CMP_BLOCK) // CMP_STRIDE + 1
    idx = jnp.arange(n_cmp)[:, None] * CMP_STRIDE + jnp.arange(CMP_BLOCK)[None, :]

    def compress(t, pos_emb, w1, w2):
        blk = t[:, idx] + pos_emb[:, None, :]
        blk = blk.transpose(0, 1, 3, 2, 4).reshape(B, n_cmp, N_KV_GROUPS, CMP_BLOCK * HEAD_DIM)
        return jax.nn.gelu(blk @ w1) @ w2

    k_cmp = compress(k_ct, cmp_pos_k, cmp_k_w1, cmp_k_w2)
    v_cmp = compress(v_ct, cmp_pos_v, cmp_v_w1, cmp_v_w2)
    return (k_cmp, v_cmp, k_slc, v_slc, k_win, v_win)

def nsa_attention(xn, w_q, w_o, rel_bias, k_cmp, v_cmp, k_slc, v_slc, k_win, v_win):
    B, S, _ = xn.shape
    G, R, Dh = N_KV_GROUPS, GROUP, HEAD_DIM
    dt = xn.dtype
    proj = xn @ w_q
    q = proj[..., :N_HEADS * Dh].reshape(B, S, G, R, Dh) * (Dh ** -0.5)
    gates = jax.nn.sigmoid(proj[..., N_HEADS * Dh:].reshape(B, S, 3, G, R))
    pos = jnp.arange(S, dtype=jnp.int32)
    tbl = rel_bias.reshape(N_BUCKETS, G, R)

    n_cmp = k_cmp.shape[1]
    cmp_start = jnp.arange(n_cmp, dtype=jnp.int32) * CMP_STRIDE
    dist_c = pos[:, None] - (cmp_start + CMP_BLOCK - 1)[None, :]
    bias_c = tbl[rel_bucket(dist_c)].transpose(2, 3, 0, 1)
    s_c = jnp.einsum('bsgrd,bcgd->bgrsc', q, k_cmp) + bias_c
    p_c = masked_softmax(s_c, dist_c >= 0)
    o_cmp = jnp.einsum('bgrsc,bcgd->bsgrd', p_c.astype(dt), v_cmp)

    n_slc = S // SLC_BLOCK
    n_sel = min(N_SELECT, n_slc)
    slc_start = jnp.arange(n_slc, dtype=jnp.int32) * SLC_BLOCK
    overlap = ((cmp_start[:, None] < slc_start[None, :] + SLC_BLOCK) &
               (cmp_start[:, None] + CMP_BLOCK > slc_start[None, :])).astype(jnp.float32)
    imp = jnp.einsum('bgrsc,cj->bsgj', p_c, overlap)
    q_blk = (pos // SLC_BLOCK)[:, None]
    j = jnp.arange(n_slc, dtype=jnp.int32)[None, :]
    valid = (j <= q_blk)[:, None, :]
    forced = ((j == 0) | (j == q_blk) | (j == q_blk - 1))[:, None, :]
    score = jnp.where(forced, 1e9, jnp.where(valid, imp, -1e9))
    _, sel = lax.top_k(score, n_sel)

    n_qb = S // Q_BLOCK
    kb = k_slc.reshape(B, n_slc, SLC_BLOCK, G, Dh).transpose(0, 3, 1, 2, 4)
    vb = v_slc.reshape(B, n_slc, SLC_BLOCK, G, Dh).transpose(0, 3, 1, 2, 4)
    kw_pad = jnp.pad(k_win, ((0, 0), (WINDOW, 0), (0, 0), (0, 0)))
    vw_pad = jnp.pad(v_win, ((0, 0), (WINDOW, 0), (0, 0), (0, 0)))
    bi = jnp.arange(B)[:, None, None, None]
    gi = jnp.arange(G)[None, None, :, None]
    gi5 = gi[..., None]
    offs = jnp.arange(SLC_BLOCK, dtype=jnp.int32)
    band = jnp.arange(WINDOW + Q_BLOCK, dtype=jnp.int32)
    n_sel_tok = n_sel * SLC_BLOCK

    def block_fn(args):
        qb, selb, t0 = args
        tq = t0 + jnp.arange(Q_BLOCK, dtype=jnp.int32)
        ks = kb[bi, gi, selb]
        vs = vb[bi, gi, selb]
        dist_s = tq[None, :, None, None, None] - (selb[..., None] * SLC_BLOCK + offs)
        bias_s = tbl[rel_bucket(dist_s), gi5].transpose(0, 1, 2, 5, 3, 4)
        s_s = jnp.einsum('bqgrd,bqgnkd->bqgrnk', qb, ks) + bias_s
        s_s = s_s.reshape(B, Q_BLOCK, G, R, n_sel_tok)
        mask_s = (dist_s >= 0).reshape(B, Q_BLOCK, G, 1, n_sel_tok)
        p_s = masked_softmax(s_s, mask_s)
        o_s = jnp.einsum('bqgrk,bqgkd->bqgrd', p_s.astype(dt), vs.reshape(B, Q_BLOCK, G, n_sel_tok, Dh))

        kw = lax.dynamic_slice_in_dim(kw_pad, t0, WINDOW + Q_BLOCK, axis=1)
        vw = lax.dynamic_slice_in_dim(vw_pad, t0, WINDOW + Q_BLOCK, axis=1)
        kpos = t0 - WINDOW + band
        dist_w = tq[:, None] - kpos[None, :]
        mask_w = (dist_w >= 0) & (dist_w < WINDOW) & (kpos[None, :] >= 0)
        bias_w = tbl[rel_bucket(dist_w)].transpose(0, 2, 3, 1)
        s_w = jnp.einsum('bqgrd,bkgd->bqgrk', qb, kw) + bias_w
        p_w = masked_softmax(s_w, mask_w[:, None, None, :])
        o_w = jnp.einsum('bqgrk,bkgd->bqgrd', p_w.astype(dt), vw)
        return o_s, o_w

    q_blocks = jnp.moveaxis(q.reshape(B, n_qb, Q_BLOCK, G, R, Dh), 1, 0)
    sel_blocks = jnp.moveaxis(sel.reshape(B, n_qb, Q_BLOCK, G, n_sel), 1, 0)
    t0s = jnp.arange(n_qb, dtype=jnp.int32) * Q_BLOCK
    o_s, o_w = lax.map(block_fn, (q_blocks, sel_blocks, t0s))
    o_s = jnp.moveaxis(o_s, 0, 1).reshape(B, S, G, R, Dh)
    o_w = jnp.moveaxis(o_w, 0, 1).reshape(B, S, G, R, Dh)

    o = (gates[:, :, 0, :, :, None] * o_cmp + gates[:, :, 1, :, :, None] * o_s
         + gates[:, :, 2, :, :, None] * o_w)
    return o.reshape(B, S, N_HEADS * Dh) @ w_o

def setup_inputs(seed: int = 0) -> dict:
    key = jax.random.key(seed)
    keys = iter(jax.random.split(key, 48))
    f32 = jnp.float32

    def w(shape, fan_in):
        return jax.random.normal(next(keys), shape, f32) * (fan_in ** -0.5)

    def gain(shape):
        return 1.0 + 0.05 * jax.random.normal(next(keys), shape, f32)

    def small(shape, scale=0.01):
        return scale * jax.random.normal(next(keys), shape, f32)

    lru_s = jax.random.uniform(next(keys), (N_A_LAYERS, D_RNN), f32, 0.9, 0.999) ** (1.0 / LRU_C)
    d_q = N_HEADS * HEAD_DIM + 3 * N_HEADS
    return {
        'x': jax.random.normal(next(keys), (BATCH, SEQ, D_MODEL), f32),
        'p': jax.random.normal(next(keys), (DEPTH, BATCH, SEQ, D_PLE), f32),
        'g_mix': gain((DEPTH, D_MODEL)),
        'g_ffn': gain((DEPTH, D_MODEL)),
        'g_ple': gain((DEPTH, D_MODEL)),
        'g_final': gain((D_MODEL,)),
        'rg_w_in': w((N_A_LAYERS, D_MODEL, 2 * D_RNN), D_MODEL),
        'rg_conv_w': w((N_A_LAYERS, CONV_WIDTH, D_RNN), CONV_WIDTH),
        'rg_conv_b': small((N_A_LAYERS, D_RNN)),
        'rg_w_a': w((N_A_LAYERS, LRU_BLOCKS, LRU_BLOCK_W, LRU_BLOCK_W), LRU_BLOCK_W),
        'rg_b_a': small((N_A_LAYERS, D_RNN)),
        'rg_w_x': w((N_A_LAYERS, LRU_BLOCKS, LRU_BLOCK_W, LRU_BLOCK_W), LRU_BLOCK_W),
        'rg_b_x': small((N_A_LAYERS, D_RNN)),
        'rg_lambda': jnp.log(lru_s) - jnp.log1p(-lru_s),
        'rg_w_out': w((N_A_LAYERS, D_RNN, D_MODEL), D_RNN),
        'kv_norm': gain((D_MODEL,)),
        'w_kv': w((D_MODEL, N_KV_BRANCH * N_KV_GROUPS * HEAD_DIM), D_MODEL),
        'cmp_pos_k': small((CMP_BLOCK, HEAD_DIM), 0.1),
        'cmp_pos_v': small((CMP_BLOCK, HEAD_DIM), 0.1),
        'cmp_k_w1': w((CMP_BLOCK * HEAD_DIM, CMP_HIDDEN), CMP_BLOCK * HEAD_DIM),
        'cmp_k_w2': w((CMP_HIDDEN, HEAD_DIM), CMP_HIDDEN),
        'cmp_v_w1': w((CMP_BLOCK * HEAD_DIM, CMP_HIDDEN), CMP_BLOCK * HEAD_DIM),
        'cmp_v_w2': w((CMP_HIDDEN, HEAD_DIM), CMP_HIDDEN),
        'rel_bias': small((N_BUCKETS, N_HEADS), 0.3),
        'nsa_w_q': w((N_B_LAYERS, D_MODEL, d_q), D_MODEL),
        'nsa_w_o': w((N_B_LAYERS, N_HEADS * HEAD_DIM, D_MODEL), N_HEADS * HEAD_DIM),
        'ffn_w_gu': w((N_DENSE, D_MODEL, 2 * D_FF), D_MODEL),
        'ffn_w_down': w((N_DENSE, D_FF, D_MODEL), D_FF),
        'moe_w_router': w((N_MOE, D_MODEL, N_EXPERTS), D_MODEL),
        'moe_w_gu': w((N_MOE, N_EXPERTS, D_MODEL, 2 * D_FF_EXPERT), D_MODEL),
        'moe_w_down': w((N_MOE, N_EXPERTS, D_FF_EXPERT, D_MODEL), D_FF_EXPERT),
        'ple_w_proj': w((DEPTH, D_PLE, D_MODEL), D_PLE),
        'ple_w_gate': w((DEPTH, D_MODEL, D_MODEL), D_MODEL),
    }

def reference(x, p, g_mix, g_ffn, g_ple, g_final,
              rg_w_in, rg_conv_w, rg_conv_b, rg_w_a, rg_b_a, rg_w_x, rg_b_x, rg_lambda, rg_w_out,
              kv_norm, w_kv, cmp_pos_k, cmp_pos_v, cmp_k_w1, cmp_k_w2, cmp_v_w1, cmp_v_w2, rel_bias,
              nsa_w_q, nsa_w_o, ffn_w_gu, ffn_w_down, moe_w_router, moe_w_gu, moe_w_down,
              ple_w_proj, ple_w_gate):
    shared_kv = None
    for i in range(DEPTH):
        h = rmsnorm(x, g_mix[i])
        if i < N_A_LAYERS:
            a = i
            x = x + recurrent_block(h, rg_w_in[a], rg_conv_w[a], rg_conv_b[a], rg_w_a[a], rg_b_a[a],
                                    rg_w_x[a], rg_b_x[a], rg_lambda[a], rg_w_out[a])
        else:
            b = i - N_A_LAYERS
            x = x + nsa_attention(h, nsa_w_q[b], nsa_w_o[b], rel_bias, *shared_kv)
        h = rmsnorm(x, g_ffn[i])
        if i % 2 == 0:
            x = x + swiglu(h, ffn_w_gu[i // 2], ffn_w_down[i // 2])
        else:
            x = x + moe_ffn(h, moe_w_router[i // 2], moe_w_gu[i // 2], moe_w_down[i // 2])
        ple_gate = jax.nn.sigmoid(rmsnorm(x, g_ple[i]) @ ple_w_gate[i])
        x = x + ple_gate * (p[i] @ ple_w_proj[i])
        if i == N_A_LAYERS - 1:
            shared_kv = nsa_shared_kv(x, kv_norm, w_kv, cmp_pos_k, cmp_pos_v,
                                      cmp_k_w1, cmp_k_w2, cmp_v_w1, cmp_v_w2)
    return rmsnorm(x, g_final)


_drawn_inputs = setup_inputs


def setup_inputs(seed=0):
    import zlib

    import numpy as np

    out = dict(_drawn_inputs(seed))
    spreads = {}
    factors = {'rg_b_a': 21.841, 'rg_b_x': 21.318, 'cmp_pos_k': 11.867, 'g_ple': 3.182, 'kv_norm': 3.631}
    for name, (base, spread) in spreads.items():
        noise = np.random.default_rng([zlib.crc32(name.encode()), seed]).standard_normal(out[name].shape)
        drawn = base * np.exp(spread * noise) if base else spread * noise
        out[name] = __import__('jax').numpy.asarray(drawn.astype(out[name].dtype))
    for name, factor in factors.items():
        out[name] = (out[name] * factor).astype(out[name].dtype)
    return out
```

```python
import math
from contextlib import ExitStack

import numpy as np

import concourse.bass as bass
from concourse import mybir

F32 = mybir.dt.float32
F32R = mybir.dt.float32r
I32 = mybir.dt.int32
ALU = mybir.AluOpType
ACT = mybir.ActivationFunctionType
AX = mybir.AxisListType

P = 128
D = 1024
S = 256
TB = S // P
KD = D // P
EPS = 1e-6
BANK = 512
CH = 2048
RAW = 7
SPL = 3
CONV = 4
H, G, DH = 16, 2, 64
HID = 256
NC = 15
CB, CS = 32, 16
NB = 32
FF = 3072
NFB = FF // 256
E, FE = 8, 3584
NJ = FE // BANK
EC = 6 * NJ
NITEM = 13
NEG = -1e30


def rel_bucket(dist):
    n = np.maximum(dist, 0)
    big = 16 + (np.log(np.maximum(n, 1) / 16.0) / math.log(8.0) * 16 + 1e-9).astype(np.int64)
    return np.where(n < 16, n, np.minimum(big, NB - 1))


def shape_constants():
    square = np.zeros((P, 4, P), np.float32)
    square[:, 0] = np.eye(P)
    square[:, 1] = np.triu(np.ones((P, P)), 1)
    square[:, 2] = np.arange(P)[None, :]
    square[:, 3, 0:64] = np.tril(np.ones((8, 8)), -1).reshape(-1)
    square[:, 3, 64:72] = np.arange(8)
    hot = np.zeros((NB + 1, 2, 512), np.float32)
    for way, dist in enumerate((255 - np.arange(512), np.arange(512) - 256)):
        hot[rel_bucket(dist), way, np.arange(512)] = 1.0
        hot[NB, way] = np.where(dist < 0, NEG, 0.0)
    return square, hot


C_IN = 0
C_OUT = C_IN + 8
C_FFN = C_OUT + 4
C_PP0 = C_FFN + 3 * NFB
C_PG0 = C_PP0 + 1
C_KV = C_PG0 + 4
C_W1 = C_KV + 3
C_Q = C_W1 + 4
C_QG = C_Q + 4
C_WO = C_QG + 1
C_RT = C_WO + 4
C_MOE = C_RT + 1

R_OUT, R_DOWN, R_PP0, R_PG0, R_WO, R_PP1, R_PG1 = range(1, 8)

N_MIX0, N_FFN0, N_PLE0, N_KV, N_MIX1, N_FFN1, N_PLE1, N_FIN = range(8)


def trunk(nc, x, p, g_mix, g_ffn, g_ple, g_final, rg_w_in, rg_conv_w, rg_conv_b, rg_w_a, rg_b_a, rg_w_x,
          rg_b_x, rg_lambda, rg_w_out, kv_norm, w_kv, cmp_pos_k, cmp_pos_v, cmp_k_w1, cmp_k_w2, cmp_v_w1,
          cmp_v_w2, rel_bias, nsa_w_q, nsa_w_o, ffn_w_gu, ffn_w_down, moe_w_router, moe_w_gu, moe_w_down,
          ple_w_proj, ple_w_gate, square, hot, out, upto=99):
    ctx = ExitStack()
    with ctx:
        def sb(name, shape, dt=F32, where=ctx):
            return where.enter_context(nc.sbuf_tensor(name, shape, dt))

        def sem(name):
            return ctx.enter_context(nc.semaphore(name))

        raw = sb("raw", [P, RAW, CH])
        whi = sb("whi", [P, SPL, CH], F32R)
        wlo = sb("wlo", [P, SPL, CH], F32R)
        X = sb("X", [P, TB, D])
        xn = sb("xn", [P, TB, D])
        xTh = sb("xTh", [P, KD, S], F32R)
        xTl = sb("xTl", [P, KD, S], F32R)
        gain = sb("gain", [P, 2, D])
        sq = sb("sq", [P, 4, P])
        ident, before, iota = sq[:, 0, :], sq[:, 1, :], sq[:, 2, :]
        lower8 = sq[:, 3, 0:64].rearrange("p (j i) -> p j i", j=8)
        iota8 = sq[:, 3, 64:72]
        ones = sb("ones", [P, P])
        prm = sb("prm", [P, 96])
        cbias = sb("cbias", [P, TB, H, NC])
        cmask = sb("cmask", [P, TB, NC])
        ss = sb("ss", [P, TB])
        ms = sb("ms", [P, TB])
        std = sb("std", [P, TB])
        rstd = sb("rstd", [P, TB])
        spare = sb("spare", [P, 16])

        rg = ExitStack()
        par_rows = sb("par_rows", [96, P], where=rg)
        hotv = sb("hotv", [NB + 1, 2, 512], where=rg)
        relb = sb("relb", [NB + 1, H], where=rg)
        rev = sb("rev", [H, 512], where=rg)
        bd = sb("bd", [P, 2, KD, P], where=rg)
        xrp = sb("xrp", [P, KD, S + CONV - 1], where=rg)
        xc = sb("xc", [P, KD, S], where=rg)
        r_ = sb("r_", [P, 4, S], where=rg)
        i_ = sb("i_", [P, 4, S], where=rg)
        a_ = sb("a_", [P, 4, S], where=rg)
        s_ = sb("s_", [P, 4, S], where=rg)
        gg = sb("gg", [P, KD, S], where=rg)
        lsp = sb("lsp", [P, 6, KD], where=rg)
        rg.close()
        ff = ExitStack()
        pn = sb("pn", [P, TB, 256], where=ff)
        pTh = sb("pTh", [P, 2, S], F32R, where=ff)
        pTl = sb("pTl", [P, 2, S], F32R, where=ff)
        psg = sb("psg", [P, TB, D], where=ff)
        fsg = sb("fsg", [P, 2, 2, S], where=ff)
        fh = sb("fh", [P, 2, 2, S], where=ff)
        fhh = sb("fhh", [P, 2, 2, S], F32R, where=ff)
        fhl = sb("fhl", [P, 2, 2, S], F32R, where=ff)
        ff.close()
        at = ExitStack()
        tt = sb("tt", [P, H, S], where=at)
        kd = sb("kd", [P, 2, G, S], where=at)
        vn = sb("vn", [P, 2, TB * P], where=at)
        kcd = sb("kcd", [P, G * NC], where=at)
        vcb = sb("vcb", [P, G, 4 * DH], where=at)
        qT = sb("qT", [P, KD, S], where=at)
        gt = sb("gt", [P, TB, 3 * H], where=at)
        oac = xn
        rs = sb("rs", [P, TB, 2, H], where=at)
        cf = sb("cf", [P, TB, 3, H], where=at)
        kv = ExitStack()
        kc2 = sb("kc2", [P, 2, G, S], where=kv)
        mf = sb("mf", [P, 2, CS, G, NC], where=kv)
        mh = sb("mh", [P, 2, CS, G * NC], F32R, where=kv)
        ml = sb("ml", [P, 2, CS, G * NC], F32R, where=kv)
        hid = sb("hid", [P, 2, 2, G * NC], where=kv)
        hidr = sb("hidr", [G * NC, 2, HID], where=kv)
        w2s = sb("w2s", [P, 2, 2, DH], where=kv)
        kv.close()
        sc = sb("sc", [P, H, NC], where=at)
        ec = sb("ec", [P, H, 32], where=at)
        ecT = sb("ecT", [P, 4, P], where=at)
        mxc = sb("mxc", [P, H], where=at)
        rsc = sb("rsc", [P, H], where=at)
        Ssb = sb("Ssb", [P, 2, 2, S], where=at)
        Psb = sb("Psb", [P, 2, 2, S], where=at)
        PTs = sb("PTs", [P, 2, BANK], where=at)
        nmx = sb("nmx", [P, 2, 2], where=at)
        otm = sb("otm", [P, BANK], where=at)
        at.close()
        mo = ExitStack()
        sb("embed_space", [P, 3 * 512 + TB * D], where=mo)
        xeh = sb("xeh", [P, KD, P], F32R, where=mo)
        xel = sb("xel", [P, KD, P], F32R, where=mo)
        Pm = sb("Pm", [P, TB, P], where=mo)
        PmT = sb("PmT", [P, S], where=mo)
        osb = sb("osb", [P, D], where=mo)
        msg = sb("msg", [P, BANK], where=mo)
        hm = sb("hm", [P, 2, BANK], where=mo)
        hth = sb("hth", [P, 4, P], F32R, where=mo)
        htl = sb("htl", [P, 4, P], F32R, where=mo)
        lg = sb("lg", [P, TB, E], where=mo)
        cmpa = sb("cmpa", [P, TB, E, E], where=mo)
        cmpb = sb("cmpb", [P, TB, E, E], where=mo)
        sel = sb("sel", [P, TB, E], where=mo)
        rt = sb("rt", [P, 6, TB, E], where=mo)
        posit = sb("posit", [P, TB, NITEM], where=mo)
        combo = sb("combo", [P, TB, NITEM], where=mo)
        meta = sb("meta", [P, 4], where=mo)
        metai = sb("metai", [P, 4], I32, where=mo)
        mo.close()

        ps = ctx.enter_context(nc.psum_tensor("ps", [P, 8, BANK], F32))
        scratch = nc.dram_tensor("bias_by_distance", (H, P, 384), F32, kind="Internal").ap()

        raw_in = [sem(f"raw_in{n}") for n in range(RAW)]
        hi_done = sem("hi_done")
        lo_done = sem("lo_done")
        pe_used = sem("pe_used")
        x_in = [sem(f"x_in{t}") for t in range(TB)]
        sq_in = sem("sq_in")
        par_in = sem("par_in")
        hot_in = sem("hot_in")
        bd_zero = sem("bd_zero")
        bd_in = sem("bd_in")
        relb_set = sem("relb_set")
        relb_in = sem("relb_in")
        rev_out = sem("rev_out")
        tt_in = sem("tt_in")
        w2_in = sem("w2_in")
        p_in = sem("p_in")
        gain0_in = sem("gain0_in")
        gain_in = [sem(f"gain_in{n}") for n in range(2)]
        xrp_zero = sem("xrp_zero")
        setup_ps = sem("setup_ps")
        prm_done = sem("prm_done")
        rev_done = sem("rev_done")
        cb_ps = sem("cb_ps")
        exp_lam = sem("exp_lam")
        abs_lam = sem("abs_lam")
        sp_done = sem("sp_done")
        sumsq = sem("sumsq")
        meansq = sem("meansq")
        std_done = sem("std_done")
        xn_done = sem("xn_done")
        xT_ps = sem("xT_ps")
        xTh_done = sem("xTh_done")
        xT_done = sem("xT_done")
        x_upd = sem("x_upd")
        dve_own = sem("dve_own")
        in_ps = sem("in_ps")
        xr_done = sem("xr_done")
        conv_done = sem("conv_done")
        ri_ps = sem("ri_ps")
        ri_ev = sem("ri_ev")
        at_done = sem("at_done")
        m_done = sem("m_done")
        sqrt_done = sem("sqrt_done")
        gelu_done = sem("gelu_done")
        y_done = sem("y_done")
        yh_done = sem("yh_done")
        yl_done = sem("yl_done")
        fsg_done = sem("fsg_done")
        fh_done = sem("fh_done")
        fhh_done = sem("fhh_done")
        fhl_done = sem("fhl_done")
        pT_ps = sem("pT_ps")
        pTh_done = sem("pTh_done")
        pTl_done = sem("pTl_done")
        psg_done = sem("psg_done")
        ct_ev = sem("ct_ev")
        mf_done = sem("mf_done")
        mh_done = sem("mh_done")
        ml_done = sem("ml_done")
        kd_done = sem("kd_done")
        hidr_done = sem("hidr_done")
        hid_ps = sem("hid_ps")
        hid_done = sem("hid_done")
        w2_ps = sem("w2_ps")
        kcd_done = sem("kcd_done")
        vcb_zero = sem("vcb_zero")
        vcb_done = sem("vcb_done")
        setup_ev = sem("setup_ev")
        fin_scatter = sem("fin_scatter")
        q_ps = sem("q_ps")
        q_ev = sem("q_ev")
        gt_done = sem("gt_done")
        sc_ps = sem("sc_ps")
        sc_done = sem("sc_done")
        ec_exp = sem("ec_exp")
        ec_done = sem("ec_done")
        ecT_ps = sem("ecT_ps")
        ecT_done = sem("ecT_done")
        oc_ps = sem("oc_ps")
        oc_ev = sem("oc_ev")
        S_ps = sem("S_ps")
        S_done = sem("S_done")
        nmx_done = sem("nmx_done")
        P_done = sem("P_done")
        PT_ps = sem("PT_ps")
        PT_done = sem("PT_done")
        pv_ps = sem("pv_ps")
        o_done = sem("o_done")
        oT_ps = sem("oT_ps")
        oTh_done = sem("oTh_done")
        oT_done = sem("oT_done")
        lg_done = sem("lg_done")
        lge_done = sem("lge_done")
        sel_done = sem("sel_done")
        cnt_ps = sem("cnt_ps")
        meta_done = sem("meta_done")
        p_ready = sem("p_ready")
        rows_ps = sem("rows_ps")
        m_ps = sem("m_ps")
        m_ev = sem("m_ev")
        xeh_done = sem("xeh_done")
        xe_done = sem("xe_done")
        msg_done = sem("msg_done")
        hm_done = sem("hm_done")
        t_ps = sem("t_ps")
        hth_done = sem("hth_done")
        ht_done = sem("ht_done")
        osb_done = sem("osb_done")
        y_out = sem("y_out")
        fin_done = sem("fin_done")

        HM0, HT0, OS0 = 2, 1, 1
        U_FFN0, U_PLE0, U_KV, U_FFN1 = 4, 8, 10, 14

        def cols(w, a, n):
            return w[:, a:a + n].rearrange("(k p) n -> p k n", p=P)

        def rows(w, a, n):
            return w[a * P:(a + n) * P, :].rearrange("(k p) n -> p k n", p=P)

        w_in, w_out, w_q = rg_w_in[0], rg_w_out[0], nsa_w_q[0]
        gu0, dn0 = ffn_w_gu[0], ffn_w_down[0]
        static = [cols(w_in, D + 256 * n, 256) for n in range(4)]
        static += [cols(w_in, 256 * n, 256) for n in range(4)]
        static += [rows(w_out, 2 * n, 2) for n in range(4)]
        for b in range(NFB):
            static += [cols(gu0, 256 * b, 256), cols(gu0, FF + 256 * b, 256)]
            if b:
                static.append(rows(dn0, 2 * b - 2, 2))
        static.append(rows(dn0, 2 * NFB - 2, 2))
        static.append(rows(ple_w_proj[0], 0, 2))
        static += [rows(ple_w_gate[0], 2 * n, 2) for n in range(4)]
        static += [cols(w_kv, 256 * n, 256) for n in range(3)]
        for w1 in (cmp_k_w1, cmp_v_w1):
            static += [rows(w1, 8 * n, 8) for n in range(2)]
        static += [cols(w_q, 256 * n, 256) for n in range(4)]
        static.append(cols(w_q, D, 3 * H))
        static += [rows(nsa_w_o[0], 2 * n, 2) for n in range(4)]
        static.append(moe_w_router[0].rearrange("(k p) n -> p k n", p=P))
        assert len(static) == C_MOE
        size = [c.shape[1] * c.shape[2] for c in static]
        ple1 = [rows(ple_w_proj[1], 0, 2)] + [rows(ple_w_gate[1], 2 * n, 2) for n in range(4)]

        def expert_chunks(e):
            wg = moe_w_gu[0, bass.ds(e, 1), :, :].rearrange("a (k p) n -> p (a k) n", p=P)
            wd = moe_w_down[0, bass.ds(e, 1), :, :].rearrange("a (k p) n -> p (a k) n", p=P)
            order = []
            for j in range(NJ):
                for half in range(2):
                    for o in (0, FE):
                        order.append(wg[:, 4 * half:4 * half + 4, o + BANK * j:o + BANK * (j + 1)])
                if j:
                    order += [wd[:, 4 * j - 4 + 2 * n:4 * j - 2 + 2 * n, :] for n in range(2)]
            return order + [wd[:, 4 * NJ - 4 + 2 * n:4 * NJ - 2 + 2 * n, :] for n in range(2)]

        def chunk_view(t, n, k):
            width = size[n] if n < C_MOE else CH
            return t[:, n % SPL, 0:width].rearrange("p (k n) -> p k n", k=k)

        def wait_block(eng, first, chunk0, m):
            if m % 2 == 0:
                eng.wait_ge(first, m // 2 + 1)
            else:
                eng.wait_ge(pe_used, chunk0 + m // 2 + 1)

        def wait_rows(eng, k, last_chunk, t):
            if t == 0:
                eng.wait_ge(rows_ps, k)
            else:
                eng.wait_ge(pe_used, last_chunk + 1)

        def last_gu(b):
            return C_FFN + 3 * b + (1 if b == 0 else 0)

        block = ctx.enter_context(nc.Block())

        @block.sync
        def _(sp):
            for t in range(TB):
                sp.dma_start(X[:, t, :], x[0, P * t:P * t + P, :]).then_inc(x_in[t], 16)

            def load(n, src, shift=0):
                if n >= RAW:
                    sp.wait_ge(lo_done, shift + (n - RAW + 1))
                k, w = src.shape[1], src.shape[2]
                sp.dma_start(raw[:, n % RAW, 0:k * w].rearrange("p (k n) -> p k n", k=k), src)\
                    .then_inc(raw_in[n % RAW], 16)

            for n, src in enumerate(static):
                load(n, src)
                if n == 1:
                    sp.dma_start(par_rows[0:8 * CONV, :], rg_conv_w[0].rearrange("k (c p) -> (k c) p", p=P))\
                        .then_inc(par_in, 16)
                    for v, vec in enumerate((rg_conv_b[0], rg_b_a[0], rg_b_x[0], rg_lambda[0])):
                        to = 8 * (CONV + v)
                        sp.dma_start(par_rows[to:to + 8, :], vec.rearrange("(c p) -> c p", p=P)).then_inc(par_in, 16)
                    for v, pos in enumerate((cmp_pos_k, cmp_pos_v)):
                        sp.dma_start(par_rows[64 + 16 * v:80 + 16 * v, :].rearrange("l (a d) -> l a d", a=2),
                                     pos.rearrange("(l a) d -> l a d", a=2)).then_inc(par_in, 16)
                if n == 7:
                    sp.dma_start(hotv[:, :, :], hot).then_inc(hot_in, 16)
            with sp.Fori(0, E) as e:
                for c, src in enumerate(expert_chunks(e)):
                    load(C_MOE + c, src, e * EC)
            sp.wait_ge(meta_done, 1)
            over = nc.sync.value_load(metai[0:1, 0:1], min_val=0, max_val=3)
            with sp.If(over > 0):
                with sp.Fori(0, over) as k:
                    e = nc.sync.value_load(metai[0:1, bass.ds(k + 1, 1)], min_val=0, max_val=E - 1)
                    for c, src in enumerate(expert_chunks(e)):
                        load(C_MOE + c, src, k * EC + E * EC)
            for c, src in enumerate(ple1):
                load(C_MOE + c, src, over * EC + E * EC)
            for t in range(TB):
                sp.wait_ge(fin_done, t + 1)
                sp.dma_start(out[0, P * t:P * t + P, :], xn[:, t, :]).then_inc(y_out, 16)
            sp.wait_ge(y_out, 16 * TB)

        @block.gpsimd
        def _(pool):
            nc.gpsimd.memset(bd[:, :, :, :], 0.0).then_inc(bd_zero, 1)
            nc.gpsimd.memset(relb[:, :], 1.0).then_inc(relb_set, 1)
            nc.gpsimd.memset(xrp[:, :, 0:CONV - 1], 0.0).then_inc(xrp_zero, 1)
            nc.gpsimd.memset(ones[:, :], 1.0).then_inc(relb_set, 1)
            gains = [g_mix[0], g_ffn[0], g_ple[0], kv_norm, g_mix[1], g_ffn[1], g_ple[1], g_final]

            def load_gain(n):
                if n >= 2:
                    pool.wait_ge(xn_done, 2 * (n - 1))
                src = gains[n].rearrange("(a n) -> a n", a=1).broadcast_to([P, D])
                pool.dma_start(gain[:, n % 2, :], src).then_inc(gain_in[n % 2], 16)

            pool.wait_ge(bd_zero, 1)
            for w, src in enumerate((rg_w_a, rg_w_x)):
                by_par = src[0].rearrange("(b two) i o -> two i b o", two=2)
                for par in range(2):
                    h = slice(64 * par, 64 * par + 64)
                    pool.dma_start(bd[h, w, :, h], by_par[par]).then_inc(bd_in, 16)
            pool.wait_ge(relb_set, 1)
            pool.dma_start(relb[0:NB, :], rel_bias).then_inc(relb_in, 16)
            load_gain(1)
            pool.wait_ge(rev_done, 1)
            pool.dma_start(scratch, rev[:, 0:384].unsqueeze(1).broadcast_to([H, P, 384])).then_inc(rev_out, 16)
            pool.wait_ge(x_upd, U_FFN0)
            pool.dma_start(pn[:, :, :], p[0, 0].rearrange("(t p) n -> p t n", p=P)).then_inc(p_in, 16)
            load_gain(2)
            load_gain(3)
            pool.wait_ge(x_upd, U_KV)
            nc.gpsimd.memset(vcb[:, :, :], 0.0).then_inc(vcb_zero, 1)
            pool.wait_ge(rev_out, 16)
            pool.dma_start(tt[:, :, :], bass.AP(scratch.tensor, P - 1, [[383, P], [384 * P, H], [1, S]])).then_inc(tt_in, 16)
            for w, src in enumerate((cmp_k_w2, cmp_v_w2)):
                pool.dma_start(w2s[:, w, :, :], src.rearrange("(k p) n -> p k n", p=P)).then_inc(w2_in, 16)
            load_gain(4)
            load_gain(5)
            pool.wait_ge(x_upd, U_FFN1)
            pool.dma_start(pn[:, :, :], p[1, 0].rearrange("(t p) n -> p t n", p=P)).then_inc(p_in, 16)
            load_gain(6)
            load_gain(7)

        @block.scalar
        def _(act):
            act.dma_start(sq[:, :, :], square).then_inc(sq_in, 16)
            act.dma_start(gain[:, 0, :], g_mix[0].rearrange("(a n) -> a n", a=1).broadcast_to([P, D]))\
                .then_inc(gain0_in, 16)
            done = [0]

            def split_hi(n, width=CH, shift=0, uses=0):
                act.wait_ge(raw_in[n % RAW], 16 * (n // RAW + 1) + uses)
                if n >= SPL:
                    act.wait_ge(pe_used, shift + (n - SPL + 1))
                nc.scalar.activation(whi[:, n % SPL, 0:width], raw[:, n % RAW, 0:width], ACT.Copy)\
                    .then_inc(hi_done, 1)

            def hi_to(n):
                while done[0] < n:
                    split_hi(done[0], size[done[0]] if done[0] < C_MOE else CH)
                    done[0] += 1

            warmed = [-1]

            def warm(function):
                warmed[0] += 1
                nc.scalar.activation(spare[:, warmed[0]:warmed[0] + 1], nc.const_aps.tensor(0.0, (P, 1), F32), function)

            def stats(n, sem_, counts):
                warm(ACT.Sqrt)
                for t in range(TB):
                    act.wait_ge(sem_[t], counts[t])
                    nc.scalar.activation(xn[:, t, :], X[:, t, :], ACT.Square, accum_out=ss[:, t:t + 1])\
                        .then_inc(sumsq, 1)
                    act.wait_ge(meansq, 2 * (n - 1) + t + 1)
                    nc.scalar.activation(std[:, t:t + 1], ms[:, t:t + 1], ACT.Sqrt).then_inc(std_done, 1)

            def xT_hi(n):
                for t in range(TB):
                    act.wait_ge(xT_ps, 2 * n + t + 1)
                    nc.scalar.activation(xTh[:, :, P * t:P * t + P],
                                         ps[:, 4 + 2 * t:6 + 2 * t, :].rearrange("p a (b n) -> p (a b) n", n=P),
                                         ACT.Copy).then_inc(xTh_done, 1)

            stats(1, x_in, (16, 16))
            hi_to(3)
            xT_hi(N_MIX0)
            act.wait_ge(abs_lam, 1)
            nc.scalar.activation(lsp[:, 1, :], lsp[:, 0, :], ACT.Exp).then_inc(exp_lam, 1)

            def xr(m):
                wait_block(act, in_ps, C_IN, m)
                if m == 0:
                    act.wait_ge(xrp_zero, 1)
                nc.scalar.activation(xrp[:, m, CONV - 1:], ps[:, m % 4, 0:S], ACT.Copy).then_inc(xr_done, 1)

            def gates_of(half):
                if half:
                    act.wait_ge(y_done, 1)
                for b in range(4 * half, 4 * half + 4):
                    act.wait_ge(ri_ps, b + 1)
                    for dst, at_, v in ((r_, 0, 5), (i_, S, 6)):
                        nc.scalar.activation(dst[:, b % 4, :], ps[:, 4 + b % 4, at_:at_ + S], ACT.Sigmoid,
                                             bias=prm[:, 8 * v + b:8 * v + b + 1]).then_inc(ri_ev, 1)

            def decay_of(half):
                act.wait_ge(ri_ev, 8 * half + 8)
                act.wait_ge(sp_done, 2)
                for b in range(4 * half, 4 * half + 4):
                    nc.scalar.activation(a_[:, b % 4, :], r_[:, b % 4, :], ACT.Exp, scale=lsp[:, 5, b:b + 1])
                    last = nc.scalar.activation(s_[:, b % 4, :], r_[:, b % 4, :], ACT.Tanh, scale=lsp[:, 4, b:b + 1])
                    last.then_inc(at_done, 1)

            def root_of(half):
                act.wait_ge(m_done, half + 1)
                nc.scalar.activation(s_[:, :, :], s_[:, :, :], ACT.Sqrt).then_inc(sqrt_done, 1)

            def gelu(m):
                wait_block(act, in_ps, C_IN, KD + m)
                nc.scalar.activation(gg[:, m, :], ps[:, m % 4, 0:S], ACT.Gelu_apprx_tanh).then_inc(gelu_done, 1)

            act.wait_ge(prm_done, 1)
            for m in range(6):
                hi_to(C_IN + m // 2 + 4)
                xr(m)
            hi_to(6)
            gates_of(0)
            hi_to(7)
            xr(6)
            xr(7)
            decay_of(0)
            hi_to(8)
            gelu(0)
            gelu(1)
            root_of(0)
            hi_to(9)
            gelu(2)
            gelu(3)
            gates_of(1)
            hi_to(10)
            decay_of(1)
            gelu(4)
            gelu(5)
            root_of(1)
            hi_to(11)
            gelu(6)
            gelu(7)
            for half in range(2):
                act.wait_ge(y_done, half + 1)
                nc.scalar.activation(xTh[:, 4 * half:4 * half + 4, :], gg[:, 4 * half:4 * half + 4, :], ACT.Copy)\
                    .then_inc(yh_done, 1)
            hi_to(C_FFN + 2)
            stats(2, (x_upd, x_upd), (U_FFN0 - 2, U_FFN0))
            hi_to(C_FFN + 3)
            xT_hi(N_FFN0)

            def f_silu(b):
                act.wait_ge(pe_used, last_gu(b) + 1)
                nc.scalar.activation(fsg[:, b % 2, :, :], ps[:, 4 + 2 * (b % 2):6 + 2 * (b % 2), 0:S], ACT.Silu)\
                    .then_inc(fsg_done, 1)

            def f_hi(b):
                act.wait_ge(fh_done, b + 1)
                nc.scalar.activation(fhh[:, b % 2, :, :], fh[:, b % 2, :, :], ACT.Copy).then_inc(fhh_done, 1)

            act.wait_ge(rev_out, 16)
            for b in range(NFB):
                hi_to(last_gu(b) + 4)
                f_silu(b)
                f_hi(b)
            act.wait_ge(pT_ps, 1)
            nc.scalar.activation(pTh[:, :, :], ps[:, 4, :].rearrange("p (k s) -> p k s", k=2), ACT.Copy)\
                .then_inc(pTh_done, 1)
            stats(3, (x_upd, x_upd), (U_PLE0 - 2, U_PLE0))
            hi_to(C_PP0 + 3)
            hi_to(C_PP0 + 4)
            xT_hi(N_PLE0)

            def embed_gate(k, last_chunk):
                warm(ACT.Sigmoid)
                for t in range(TB):
                    wait_rows(act, k, last_chunk, t)
                    nc.scalar.activation(psg[:, t, :], ps[:, 4 + 2 * t:6 + 2 * t, :].rearrange("p a n -> p (a n)"),
                                         ACT.Sigmoid).then_inc(psg_done, 1)

            hi_to(C_PG0 + 6)
            embed_gate(R_PG0, C_PG0 + 3)
            stats(4, (x_upd, x_upd), (U_KV - 1, U_KV))
            hi_to(C_PG0 + 7)
            xT_hi(N_KV)
            act.wait_ge(pe_used, C_KV + 1)
            for g in range(G):
                src = ps[64 * g:64 * g + 64, 1, 0:S]
                nc.scalar.activation(kc2[0:64, 1, g, :], src, ACT.Copy).then_inc(ct_ev, 1)
                nc.scalar.activation(kc2[64:128, 1, g, 0:S - 1], src[:, 1:S], ACT.Copy).then_inc(ct_ev, 1)
            act.wait_ge(pe_used, C_KV + 2)
            for g in range(G):
                for half in range(2):
                    nc.scalar.activation(kd[64 * half:64 * half + 64, 0, g, :], ps[64 * g:64 * g + 64, 2, 0:S],
                                         ACT.Copy).then_inc(kd_done, 1)
            nc.scalar.activation(vn[:, 0, :], ps[:, 3, 0:S], ACT.Copy).then_inc(kd_done, 1)
            hi_to(C_W1 + 2)
            act.wait_ge(mf_done, 1)
            nc.scalar.activation(mh[:, :, :, :], mf[:, :, :, :, :].rearrange("p a l g c -> p a l (g c)"), ACT.Copy)\
                .then_inc(mh_done, 1)
            for w in range(2):
                hi_to(C_W1 + 2 * w + 5)
                act.wait_ge(pe_used, C_W1 + 2 * w + 2)
                nc.scalar.activation(hidr[:, w, :], ps[0:G * NC, 4 - 2 * w, 0:HID], ACT.Gelu_apprx_tanh)\
                    .then_inc(hidr_done, 1)
            act.wait_ge(hid_ps, 1)
            nc.scalar.activation(hid[:, :, :, :],
                                 ps[:, 5, 0:128].rearrange("p (w k c) -> p w k c", w=2, k=2)[:, :, :, 0:G * NC],
                                 ACT.Copy).then_inc(hid_done, 1)
            act.wait_ge(w2_ps, 1)
            nc.scalar.activation(kcd[:, :], ps[:, 0, 0:G * NC], ACT.Copy).then_inc(kcd_done, 1)
            xT_hi(N_MIX1)
            for m in range(KD):
                hi_to(C_Q + m // 2 + 4)
                wait_block(act, q_ps, C_Q, m)
                nc.scalar.activation(qT[:, m, :], ps[:, m % 4, 0:S], ACT.Copy, scale=DH ** -0.5).then_inc(q_ev, 1)
            hi_to(C_QG + 4)
            act.wait_ge(pe_used, C_QG + 1)
            nc.scalar.activation(gt[:, :, :], ps[:, 4, 0:96].rearrange("p (t n) -> p t n", t=TB), ACT.Sigmoid)\
                .then_inc(gt_done, 1)
            for b in range(TB):
                act.wait_ge(sc_done, b + 1)
                nc.scalar.activation(ec[:, :, 0:NC], sc[:, :, :], ACT.Exp).then_inc(ec_exp, 1)
                act.wait_ge(ecT_ps, b + 1)
                nc.scalar.activation(ecT[:, :, :], ps[:, 2, :].rearrange("p (a n) -> p a n", n=P), ACT.Copy)\
                    .then_inc(ecT_done, 1)

            def probs_T(n):
                w = 2 * P * (n // H + 1)
                act.wait_ge(PT_ps, n + 1)
                if n >= 2:
                    act.wait_ge(pv_ps, n - 1)
                nc.scalar.activation(PTs[:, n % 2, 0:w], ps[:, 2 + n % 2, 0:w], ACT.Copy).then_inc(PT_done, 1)

            for n in range(TB * H):
                b, h = divmod(n, H)
                w = P * (b + 1)
                act.wait_ge(nmx_done, n + 1)
                if n >= 2:
                    act.wait_ge(PT_ps, n - 1)
                for br in range(2):
                    last = nc.scalar.activation(Psb[:, n % 2, br, 0:w], Ssb[:, n % 2, br, 0:w], ACT.Exp,
                                                bias=nmx[:, n % 2, br:br + 1], accum_out=rs[:, b, br, h:h + 1])
                last.then_inc(P_done, 1)
                if n:
                    probs_T(n - 1)
            probs_T(TB * H - 1)
            for t in range(TB):
                act.wait_ge(oT_ps, t + 1)
                nc.scalar.activation(xTh[:, :, P * t:P * t + P],
                                     ps[:, 2 * t:2 * t + 2, :].rearrange("p a (b n) -> p (a b) n", n=P),
                                     ACT.Copy).then_inc(oTh_done, 1)
            hi_to(C_RT + 1)
            stats(5, (x_upd, x_upd), (U_FFN1 - 2, U_FFN1))
            hi_to(C_RT + 2)
            xT_hi(N_FFN1)
            act.wait_ge(lg_done, 1)
            nc.scalar.activation(rt[:, 0, :, :], rt[:, 0, :, :], ACT.Exp).then_inc(lge_done, 1)
            hi_to(C_MOE + 3)
            for half in range(2):
                act.wait_ge(m_ps, half + 1)
                nc.scalar.activation(xeh[:, 4 * half:4 * half + 4, :],
                                     ps[:, 7, :].rearrange("p (a n) -> p a n", n=P), ACT.Copy).then_inc(xeh_done, 1)
            act.wait_ge(pT_ps, 2)
            nc.scalar.activation(pTh[:, :, :], ps[:, 2, :].rearrange("p (k s) -> p k s", k=2), ACT.Copy)\
                .then_inc(pTh_done, 1)
            act.wait_ge(meta_done, 1)
            over = nc.scalar.value_load(metai[0:1, 0:1], min_val=0, max_val=3)
            with act.Fori(0, over + E) as i:
                c0 = nc.scalar.snap(i * EC)
                uses = nc.scalar.snap(i * (16 * EC // RAW))
                i7 = nc.scalar.snap(i * 7)

                def gathered(half):
                    act.wait_ge(m_ps, i7 + (2 + 5 + half + 1))
                    act.wait_ge(pe_used, c0 + (C_MOE + 6 * NJ - 4))
                    nc.scalar.activation(xeh[:, 4 * half:4 * half + 4, :],
                                         ps[:, 7, :].rearrange("p (a n) -> p a n", n=P), ACT.Copy)\
                        .then_inc(xeh_done, 1)

                def hidden_T(j):
                    act.wait_ge(t_ps, i7 + (j + 1))
                    if j:
                        act.wait_ge(pe_used, c0 + (C_MOE + 6 * j + 4))
                    nc.scalar.activation(hth[:, :, :], ps[:, 4, :].rearrange("p (a n) -> p a n", n=P), ACT.Copy)\
                        .then_inc(hth_done, 1)

                for c in range(EC):
                    if c == EC - 3:
                        hidden_T(NJ - 1)
                        gathered(1)
                    split_hi(C_MOE + c + 3, shift=c0, uses=uses)
                    if c == 3 or (c > 3 and c % 6 == 1):
                        j = 0 if c == 3 else c // 6
                        act.wait_ge(hm_done, i7 + (HM0 + j))
                        nc.scalar.activation(msg[:, :], ps[:, 2 * (j % 2), :], ACT.Silu).then_inc(msg_done, 1)
                    if c % 6 == 5 and c // 6 < NJ - 1:
                        hidden_T(c // 6)
                    if c == 6 * NJ - 5:
                        gathered(0)
                act.wait_ge(pe_used, c0 + (C_MOE + EC))
                nc.scalar.activation(osb[:, :], ps[:, 5:7, :].rearrange("p a n -> p (a n)"), ACT.Copy)\
                    .then_inc(osb_done, 1)
            n_item = nc.scalar.snap(over + E)
            c1 = nc.scalar.snap(n_item * EC)
            uses1 = nc.scalar.snap(n_item * (16 * EC // RAW))
            stats(6, (fin_scatter, fin_scatter), (2, 4))
            split_hi(C_MOE + 3, shift=c1, uses=uses1)
            xT_hi(N_PLE1)
            split_hi(C_MOE + 4, shift=c1, uses=uses1)
            embed_gate(R_PG1, c1 + (C_MOE + 4))
            stats(7, (x_upd, x_upd), (U_FFN1 + 1, U_FFN1 + 2))

        @block.vector
        def _(dve):
            v = nc.vector
            own, done = [0], [0]

            def link(ins):
                own[0] += 1
                ins.then_inc(dve_own, 1)
                dve.wait_ge(dve_own, own[0])

            def split_lo(n, width=CH, shift=0):
                dve.wait_ge(hi_done, shift + (n + 1))
                v.tensor_tensor(wlo[:, n % SPL, 0:width], raw[:, n % RAW, 0:width],
                                whi[:, n % SPL, 0:width].bitcast(F32), ALU.subtract).then_inc(lo_done, 1)

            def lo_to(n):
                while done[0] < n:
                    split_lo(done[0], size[done[0]] if done[0] < C_MOE else CH)
                    done[0] += 1

            def norm_stats(k, t):
                dve.wait_ge(sumsq, 2 * (k - 1) + t + 1)
                v.tensor_scalar(ms[:, t:t + 1], ss[:, t:t + 1], 1.0 / D, EPS, ALU.mult, ALU.add).then_inc(meansq, 1)
                dve.wait_ge(std_done, 2 * (k - 1) + t + 1)
                link(v.reciprocal(rstd[:, t:t + 1], std[:, t:t + 1]))

            def norm_rows(n, signal, k=None):
                if n:
                    dve.wait_ge(gain_in[n % 2], 16 * ((n + 1) // 2))
                else:
                    dve.wait_ge(gain0_in, 16)
                for t in range(TB):
                    if k:
                        norm_stats(k, t)
                    v.scalar_tensor_tensor(xn[:, t, :], X[:, t, :], rstd[:, t:t + 1], gain[:, n % 2, :],
                                           ALU.mult, ALU.mult).then_inc(signal, 1)

            def xT_lo(n):
                for t in range(TB):
                    dve.wait_ge(xTh_done, 2 * n + t + 1)
                    v.tensor_tensor(xTl[:, :, P * t:P * t + P],
                                    ps[:, 4 + 2 * t:6 + 2 * t, :].rearrange("p a (b n) -> p (a b) n", n=P),
                                    xTh[:, :, P * t:P * t + P].bitcast(F32), ALU.subtract).then_inc(xT_done, 1)

            def add_block(k, last_chunk):
                for t in range(TB):
                    wait_rows(dve, k, last_chunk, t)
                    for n in range(2):
                        to = X[:, t, BANK * n:BANK * (n + 1)]
                        v.tensor_tensor(to, ps[:, 2 * t + n, :], to, ALU.add).then_inc(x_upd, 1)

            norm_rows(N_MIX0, xn_done, 1)
            lo_to(2)
            xT_lo(N_MIX0)
            lo_to(3)
            dve.wait_ge(setup_ps, 1)
            v.tensor_copy(prm[:, :], ps[:, 4, 0:96]).then_inc(prm_done, 1)
            dve.wait_ge(prm_done, 1)
            lam = prm[:, 56:64]
            v.scalar_tensor_tensor(lsp[:, 0, :], lam, -1.0, lam, ALU.mult, ALU.min).then_inc(abs_lam, 1)
            dve.wait_ge(exp_lam, 1)
            y, z, z2, q = (lsp[:, n, :] for n in (1, 2, 3, 4))
            link(v.tensor_scalar(z, y, 2.0, None, ALU.add))
            link(v.reciprocal(z, z))
            link(v.tensor_tensor(z, y, z, ALU.mult))
            link(v.tensor_tensor(z2, z, z, ALU.mult))
            link(v.tensor_scalar(q, z2, 1.0 / 17, None, ALU.mult))
            for k in (15, 13, 11, 9, 7, 5, 3):
                link(v.scalar_tensor_tensor(q, q, 1.0 / k, z2, ALU.add, ALU.mult))
            link(v.scalar_tensor_tensor(q, q, 1.0, z, ALU.add, ALU.mult))
            link(v.tensor_scalar(lsp[:, 0, :], lam, -1.0, 0.0, ALU.mult, ALU.max))
            link(v.scalar_tensor_tensor(q, q, 2.0, lsp[:, 0, :], ALU.mult, ALU.add))
            v.tensor_scalar(lsp[:, 5, :], q, -8.0, None, ALU.mult).then_inc(sp_done, 1)
            dve.wait_ge(sp_done, 1)
            v.tensor_scalar(lsp[:, 4, :], q, 8.0, None, ALU.mult).then_inc(sp_done, 1)

            def conv(m):
                dve.wait_ge(xr_done, m + 1)
                link(v.tensor_scalar(xc[:, m, :], xrp[:, m, 0:S], prm[:, m:m + 1], prm[:, 32 + m:33 + m],
                                     ALU.mult, ALU.add))
                for k in range(1, CONV):
                    last = v.scalar_tensor_tensor(xc[:, m, :], xrp[:, m, k:k + S], prm[:, 8 * k + m:8 * k + m + 1],
                                                  xc[:, m, :], ALU.mult, ALU.add)
                    if k < CONV - 1:
                        link(last)
                last.then_inc(conv_done, 1)

            def recur(half):
                hs = slice(4 * half, 4 * half + 4)
                dve.wait_ge(at_done, 4 * half + 4)
                link(v.tensor_tensor(r_[:, :, :], a_[:, :, :], a_[:, :, :], ALU.mult))
                v.scalar_tensor_tensor(s_[:, :, :], r_[:, :, :], 1.0, s_[:, :, :], ALU.add, ALU.mult).then_inc(m_done, 1)
                link(v.tensor_tensor(i_[:, :, :], i_[:, :, :], xc[:, hs, :], ALU.mult))
                dve.wait_ge(sqrt_done, half + 1)
                link(v.tensor_tensor(i_[:, :, :], s_[:, :, :], i_[:, :, :], ALU.mult))
                for b in range(4):
                    last = v.tensor_tensor_scan(r_[:, b, :], a_[:, b, :], i_[:, b, :], 0.0, ALU.mult, ALU.add)
                link(last)
                dve.wait_ge(gelu_done, 4 * half + 4)
                v.tensor_tensor(gg[:, hs, :], gg[:, hs, :], r_[:, :, :], ALU.mult).then_inc(y_done, 1)

            for m in range(8):
                lo_to(C_IN + m // 2 + 4)
                conv(m)
            lo_to(8)
            recur(0)
            lo_to(10)
            recur(1)
            dve.wait_ge(setup_ps, 2)
            v.tensor_copy(rev[:, :], ps[0:H, 4, :]).then_inc(rev_done, 1)
            dve.wait_ge(setup_ps, 3)
            link(v.tensor_copy(cbias[:, :, :, :],
                               ps[:, 5, 0:TB * NC * H].rearrange("p (b c h) -> p b h c", b=TB, c=NC)))
            v.tensor_scalar(cmask[:, :, :], cbias[:, :, 0, :], NEG / 10, None, ALU.is_gt).then_inc(setup_ev, 1)
            lo_to(11)
            for half in range(2):
                hs = slice(4 * half, 4 * half + 4)
                dve.wait_ge(yh_done, half + 1)
                v.tensor_tensor(xTl[:, hs, :], gg[:, hs, :], xTh[:, hs, :].bitcast(F32), ALU.subtract)\
                    .then_inc(yl_done, 1)
            lo_to(C_FFN + 2)
            add_block(R_OUT, C_OUT + 3)
            norm_rows(N_FFN0, xn_done, 2)
            lo_to(C_FFN + 3)
            xT_lo(N_FFN0)

            def f_mul(b):
                dve.wait_ge(fsg_done, b + 1)
                v.tensor_tensor(fh[:, b % 2, :, :], ps[:, 4 + 2 * (b % 2):6 + 2 * (b % 2), S:2 * S],
                                fsg[:, b % 2, :, :], ALU.mult).then_inc(fh_done, 1)

            def f_lo(b):
                dve.wait_ge(fhh_done, b + 1)
                v.tensor_tensor(fhl[:, b % 2, :, :], fh[:, b % 2, :, :], fhh[:, b % 2, :, :].bitcast(F32),
                                ALU.subtract).then_inc(fhl_done, 1)

            for b in range(NFB):
                lo_to(last_gu(b) + 4)
                f_mul(b)
                f_lo(b)

            def p_lo(k, bank):
                dve.wait_ge(pTh_done, k)
                v.tensor_tensor(pTl[:, :, :], ps[:, bank, :].rearrange("p (k s) -> p k s", k=2),
                                pTh[:, :, :].bitcast(F32), ALU.subtract).then_inc(pTl_done, 1)

            def embed(k):
                for t in range(TB):
                    dve.wait_ge(psg_done, TB * (k - 1) + t + 1)
                    link(v.tensor_tensor(psg[:, t, :], ps[:, 2 * t:2 * t + 2, :].rearrange("p a n -> p (a n)"),
                                         psg[:, t, :], ALU.mult))
                    v.tensor_tensor(X[:, t, :], psg[:, t, :], X[:, t, :], ALU.add).then_inc(x_upd, 1)

            p_lo(1, 4)
            lo_to(C_PP0 + 1)
            add_block(R_DOWN, C_PP0 - 1)
            norm_rows(N_PLE0, xn_done, 3)
            lo_to(C_PP0 + 3)
            lo_to(C_PP0 + 4)
            xT_lo(N_PLE0)
            lo_to(C_PG0 + 6)
            embed(1)
            norm_rows(N_KV, xn_done, 4)
            lo_to(C_PG0 + 7)
            xT_lo(N_KV)
            dve.wait_ge(pe_used, C_KV + 1)
            for g in range(G):
                src = ps[64 * g:64 * g + 64, 0, 0:S]
                v.tensor_copy(kc2[0:64, 0, g, :], src).then_inc(ct_ev, 1)
                v.tensor_copy(kc2[64:128, 0, g, 0:S - 1], src[:, 1:S]).then_inc(ct_ev, 1)
            dve.wait_ge(ct_ev, 8)
            for w in range(2):
                view = bass.AP(kc2, w * G * S, [[2 * G * S, P], [2, CS], [S, G], [CS, NC]])
                pos = prm[:, 64 + CS * w:64 + CS * (w + 1)]
                pos = bass.AP(pos.tensor, pos.offset, [list(pos.ap[0]), [1, CS], [0, G], [0, NC]])
                last = v.tensor_tensor(mf[:, w, :, :, :], view, pos, ALU.add)
            last.then_inc(mf_done, 1)
            lo_to(C_W1 + 1)
            dve.wait_ge(mh_done, 1)
            v.tensor_tensor(ml[:, :, :, :], mf[:, :, :, :, :].rearrange("p a l g c -> p a l (g c)"),
                            mh[:, :, :, :].bitcast(F32), ALU.subtract).then_inc(ml_done, 1)
            dve.wait_ge(pe_used, C_KV + 3)
            for g in range(G):
                for half in range(2):
                    v.tensor_copy(kd[64 * half:64 * half + 64, 1, g, :], ps[64 * g:64 * g + 64, 6, 0:S])\
                        .then_inc(kd_done, 1)
            v.tensor_copy(vn[:, 1, :], ps[:, 7, 0:S]).then_inc(kd_done, 1)
            lo_to(C_W1 + 5)
            norm_rows(N_MIX1, xn_done)
            lo_to(C_W1 + 7)
            dve.wait_ge(w2_ps, 2)
            dve.wait_ge(vcb_zero, 1)
            for g in range(G):
                for a in range(4):
                    v.tensor_copy(vcb[32 * a:32 * a + NC, g, DH * a:DH * (a + 1)],
                                  ps[0:NC, 1, DH * g:DH * (g + 1)]).then_inc(vcb_done, 1)
            xT_lo(N_MIX1)
            lo_to(C_QG + 4)

            def by_head(a, width):
                return a.unsqueeze(2).broadcast_to([P, a.shape[1], width])

            for b in range(TB):
                dve.wait_ge(sc_ps, b + 1)
                if b == 0:
                    v.memset(ec[:, :, :], 0.0)
                for par in range(2):
                    view = sc[:, :, :].rearrange("p (a two) c -> p a two c", two=2)[:, :, par, :]
                    bias = cbias[:, b, :, :].rearrange("p (a two) c -> p a two c", two=2)[:, :, par, :]
                    link(v.tensor_tensor(view, ps[:, par, 0:8 * NC].rearrange("p (a c) -> p a c", c=NC), bias, ALU.add))
                link(v.tensor_reduce(mxc[:, :], sc[:, :, :], AX.X, ALU.max))
                v.tensor_tensor(sc[:, :, :], sc[:, :, :], by_head(mxc[:, :], NC), ALU.subtract).then_inc(sc_done, 1)
                dve.wait_ge(ec_exp, b + 1)
                keep = cmask[:, b, :].unsqueeze(1).broadcast_to([P, H, NC])
                v.tensor_tensor(ec[:, :, 0:NC], ec[:, :, 0:NC], keep, ALU.mult).then_inc(ec_done, 1)
                dve.wait_ge(ec_done, b + 1)
                link(v.tensor_reduce(rsc[:, :], ec[:, :, 0:NC], AX.X, ALU.add))
                link(v.tensor_scalar(rsc[:, :], rsc[:, :], 1e-30, None, ALU.max))
                link(v.reciprocal(rsc[:, :], rsc[:, :]))
                dve.wait_ge(gt_done, 1)
                link(v.tensor_tensor(cf[:, b, 0, :], rsc[:, :], gt[:, b, 0:H], ALU.mult))
                dve.wait_ge(oc_ps, b + 1)
                for n in range(2):
                    v.tensor_tensor(oac[:, b, BANK * n:BANK * (n + 1)].rearrange("p (h d) -> p h d", d=DH),
                                    ps[:, 4 + 2 * b + n, :].rearrange("p (h d) -> p h d", d=DH),
                                    by_head(cf[:, b, 0, 8 * n:8 * n + 8], DH), ALU.mult).then_inc(oc_ev, 1)

            def combine(b):
                dve.wait_ge(P_done, H * (b + 1))
                link(v.reciprocal(cf[:, b, 1:3, :], rs[:, b, :, :]))
                link(v.tensor_tensor(cf[:, b, 1:3, :], cf[:, b, 1:3, :],
                                     gt[:, b, H:3 * H].rearrange("p (a h) -> p a h", a=2), ALU.mult))
                dve.wait_ge(pv_ps, H * (b + 1))
                dve.wait_ge(oc_ev, 2 * b + 2)
                for br in range(2):
                    for k in range(2):
                        link(v.tensor_tensor(otm[:, :].rearrange("p (h d) -> p h d", d=DH),
                                             ps[:, 4 + 2 * br + k, :].rearrange("p (h d) -> p h d", d=DH),
                                             by_head(cf[:, b, 1 + br, 8 * k:8 * k + 8], DH), ALU.mult))
                        to = oac[:, b, BANK * k:BANK * (k + 1)]
                        last = v.tensor_tensor(to, otm[:, :], to, ALU.add)
                        if br == 1 and k == 1:
                            last.then_inc(o_done, 1)
                        else:
                            link(last)

            dve.wait_ge(tt_in, 16)
            for n in range(TB * H):
                b, h = divmod(n, H)
                w = P * (b + 1)
                dve.wait_ge(S_ps, n + 1)
                if n >= 2:
                    dve.wait_ge(P_done, n - 1)
                bias = tt[:, h, S - w:S].unsqueeze(1).broadcast_to([P, 2, w])
                v.tensor_tensor(Ssb[:, n % 2, :, 0:w],
                                ps[:, n % 2, :].rearrange("p (r s) -> p r s", r=2)[:, :, 0:w],
                                bias, ALU.add).then_inc(S_done, 1)
                dve.wait_ge(S_done, n + 1)
                v.tensor_reduce(nmx[:, n % 2, :], Ssb[:, n % 2, :, 0:w], AX.X, ALU.max, negate=True)\
                    .then_inc(nmx_done, 1)
                if n == H:
                    combine(0)
            combine(1)
            for t in range(TB):
                dve.wait_ge(oTh_done, t + 1)
                v.tensor_tensor(xTl[:, :, P * t:P * t + P],
                                ps[:, 2 * t:2 * t + 2, :].rearrange("p a (b n) -> p (a b) n", n=P),
                                xTh[:, :, P * t:P * t + P].bitcast(F32), ALU.subtract).then_inc(oT_done, 1)
            lo_to(C_RT + 1)
            add_block(R_WO, C_WO + 3)
            norm_rows(N_FFN1, xn_done, 5)
            lo_to(C_RT + 2)
            xT_lo(N_FFN1)
            v.memset(posit[:, :, :], -1.0)
            link(v.memset(combo[:, :, :], 0.0))
            v.memset(osb[:, :], 0.0).then_inc(osb_done, OS0)
            v.memset(PmT[:, :], 0.0).then_inc(ht_done, HT0)
            dve.wait_ge(pe_used, C_RT + 1)
            link(v.tensor_copy(lg[:, :, :], ps[:, 0, 0:TB * E].rearrange("p (t e) -> p t e", t=TB)))
            top, total = rt[:, 5, 0, 0:TB], rt[:, 5, 1, 0:TB]
            link(v.tensor_reduce(top, lg[:, :, :], AX.X, ALU.max))
            v.tensor_tensor(rt[:, 0, :, :], lg[:, :, :], top.unsqueeze(2).broadcast_to([P, TB, E]), ALU.subtract)\
                .then_inc(lg_done, 1)
            rank = rt[:, 1, :, :]
            for t in range(TB):
                li = lg[:, t, :].unsqueeze(1).broadcast_to([P, E, E])
                lj = lg[:, t, :].unsqueeze(2).broadcast_to([P, E, E])
                link(v.tensor_tensor(cmpa[:, t, :, :], li, lj, ALU.is_gt))
                link(v.tensor_tensor(cmpb[:, t, :, :], li, lj, ALU.is_equal))
                link(v.tensor_tensor(cmpb[:, t, :, :], cmpb[:, t, :, :], lower8, ALU.mult))
                link(v.tensor_tensor(cmpa[:, t, :, :], cmpa[:, t, :, :], cmpb[:, t, :, :], ALU.add))
            link(v.tensor_reduce(rank, cmpa[:, :, :, :], AX.X, ALU.add))
            v.tensor_scalar(sel[:, :, :], rank, 2.0, None, ALU.is_lt).then_inc(sel_done, 1)
            dve.wait_ge(sel_done, 1)
            dve.wait_ge(lge_done, 1)
            comb = rt[:, 2, :, :]
            link(v.tensor_tensor(comb, rt[:, 0, :, :], sel[:, :, :], ALU.mult))
            link(v.tensor_reduce(total, comb, AX.X, ALU.add))
            link(v.reciprocal(total, total))
            link(v.tensor_tensor(comb, comb, total.unsqueeze(2).broadcast_to([P, TB, E]), ALU.mult))
            link(v.tensor_copy(combo[:, :, 1:1 + E], comb))
            dve.wait_ge(cnt_ps, 1)
            slot = rt[:, 3, :, :]
            link(v.scalar_tensor_tensor(slot, ps[:, 1, 0:TB * E].rearrange("p (t e) -> p t e", t=TB), 1.0,
                                        sel[:, :, :], ALU.add, ALU.mult))
            link(v.tensor_scalar(slot, slot, -1.0, None, ALU.add))
            link(v.tensor_copy(posit[:, :, 1:1 + E], slot))
            full, nth = rt[:, 4, 0, :], rt[:, 4, 1, :]
            link(v.tensor_scalar(full, ps[:, 1, TB * E:(TB + 1) * E], float(P), None, ALU.is_gt))
            link(v.tensor_tensor(cmpa[:, 0, :, :], full.unsqueeze(1).broadcast_to([P, E, E]), lower8, ALU.mult))
            link(v.tensor_reduce(nth, cmpa[:, 0, :, :], AX.X, ALU.add))
            link(v.tensor_reduce(meta[:, 0:1], full, AX.X, ALU.add))
            pick, part = rt[:, 1, 0, :], cmpb[:, :, 0, :]
            for k in range(3):
                at_ = 1 + E + k
                wide = pick.unsqueeze(1).broadcast_to([P, TB, E])
                link(v.scalar_tensor_tensor(pick, nth, float(k), full, ALU.is_equal, ALU.mult))
                link(v.tensor_tensor(part, slot, wide, ALU.mult))
                link(v.tensor_reduce(posit[:, :, at_:at_ + 1], part, AX.X, ALU.add))
                link(v.tensor_scalar(posit[:, :, at_:at_ + 1], posit[:, :, at_:at_ + 1], -float(P), None, ALU.add))
                link(v.tensor_tensor(part, comb, wide, ALU.mult))
                link(v.tensor_reduce(combo[:, :, at_:at_ + 1], part, AX.X, ALU.add))
                link(v.tensor_tensor(part[:, 0, :], pick, iota8, ALU.mult))
                link(v.tensor_reduce(meta[:, 1 + k:2 + k], part[:, 0, :], AX.X, ALU.add))
            v.tensor_copy(metai[:, :], meta[:, :]).then_inc(meta_done, 1)
            for t in range(TB):
                last = v.tensor_scalar(Pm[:, t, :], iota, posit[:, t, 1:2], None, ALU.is_equal)
            last.then_inc(p_ready, 1)
            lo_to(C_MOE + 3)

            def tokens_lo(half):
                last = v.tensor_tensor(xel[:, 4 * half:4 * half + 4, :], ps[:, 7, :].rearrange("p (a n) -> p a n", n=P),
                                       xeh[:, 4 * half:4 * half + 4, :].bitcast(F32), ALU.subtract)
                last.then_inc(m_ev, 1)

            for half in range(2):
                dve.wait_ge(xeh_done, half + 1)
                tokens_lo(half)
            p_lo(2, 2)
            v.memset(hm[:, :, :], 0.0).then_inc(hm_done, HM0)
            dve.wait_ge(meta_done, 1)
            over = v.value_load(metai[0:1, 0:1], min_val=0, max_val=3)

            def add_scatter(k, item, bank=7):
                t, n = divmod(k, 2)
                to = X[:, t, BANK * n:BANK * (n + 1)]
                return v.scalar_tensor_tensor(to, ps[:, bank, :], combo[:, t, bass.ds(item, 1)], to, ALU.mult, ALU.add)

            with dve.Fori(0, over + E) as i:
                c0 = v.snap(i * EC)
                i7 = v.snap(i * 7)

                def hidden_lo(j):
                    dve.wait_ge(hth_done, i7 + (j + 1))
                    v.tensor_tensor(htl[:, :, :], ps[:, 4, :].rearrange("p (a n) -> p a n", n=P),
                                    hth[:, :, :].bitcast(F32), ALU.subtract).then_inc(ht_done, 1)

                def gathered_lo(half):
                    dve.wait_ge(xeh_done, i * 2 + (2 + half + 1))
                    tokens_lo(half)

                for c in range(EC):
                    if c == EC - 3:
                        hidden_lo(NJ - 1)
                        gathered_lo(1)
                    split_lo(C_MOE + c + 3, shift=c0)
                    if c in (1, 3, 5, 7):
                        dve.wait_ge(m_ps, i7 + (2 + c // 2 + 1))
                        add_scatter(c // 2, i).then_inc(m_ev, 1)
                    if c == 3 or (c > 3 and c % 6 == 1):
                        j = 0 if c == 3 else c // 6
                        dve.wait_ge(msg_done, i7 + (j + 1))
                        v.tensor_tensor(hm[:, j % 2, :], ps[:, 2 * (j % 2) + 1, :], msg[:, :], ALU.mult)\
                            .then_inc(hm_done, 1)
                    if c == 9:
                        dve.wait_ge(m_ps, i7 + (2 + 4 + 1))
                        v.tensor_copy(PmT[:, :], ps[:, 7, 0:S]).then_inc(m_ev, 1)
                        for t in range(TB):
                            last = v.tensor_scalar(Pm[:, t, :], iota, posit[:, t, bass.ds(i + 2, 1)], None, ALU.is_equal)
                        last.then_inc(p_ready, 1)
                    if c % 6 == 5 and c // 6 < NJ - 1:
                        hidden_lo(c // 6)
                    if c == 6 * NJ - 5:
                        gathered_lo(0)
            n_item = v.snap(over + E)
            m0 = v.snap(n_item * 7)
            for k in range(4):
                dve.wait_ge(m_ps, m0 + (2 + k + 1))
                add_scatter(k, n_item, 7 - k).then_inc(fin_scatter, 1)
            c1 = v.snap(n_item * EC)
            norm_rows(N_PLE1, xn_done, 6)
            split_lo(C_MOE + 3, shift=c1)
            xT_lo(N_PLE1)
            split_lo(C_MOE + 4, shift=c1)
            embed(2)
            norm_rows(N_FIN, fin_done, 7)

        @block.tensor
        def _(pe):
            mm = nc.tensor.matmul

            def mm3(to, sh, sl, mh_, ml_, start, stop):
                mm(to, sh, mh_, start=start, stop=False)
                mm(to, sh, ml_, start=False, stop=False)
                return mm(to, sl, mh_, start=False, stop=stop)

            def arrive(n, k, shift=0):
                pe.wait_ge(lo_done, shift + (n + 1))
                return chunk_view(whi, n, k), chunk_view(wlo, n, k)

            def norm_T(n):
                for t in range(TB):
                    pe.wait_ge(xn_done, 2 * n + t + 1)
                    for k in range(KD):
                        last = nc.tensor.transpose(ps[:, 4 + 2 * t + k // 4, P * (k % 4):P * (k % 4) + P],
                                                   xn[:, t, P * k:P * k + P], ident)
                    last.then_inc(xT_ps, 1)

            def transposed_product(n, m, to):
                wh, wl = chunk_view(whi, n, KD), chunk_view(wlo, n, KD)
                cs = slice(P * m, P * m + P)
                for k in range(KD):
                    a, z = k == 0, k == KD - 1
                    mm(to, wh[:, k, cs], xTh[:, k, :], start=a, stop=False)
                    mm(to, wh[:, k, cs], xTl[:, k, :], start=False, stop=False)
                    last = mm(to, wl[:, k, cs], xTh[:, k, :], start=False, stop=z)
                return last

            def rows_product(n, k0, bank0, sh, sl, first, last_k, shift=0):
                wh, wl = arrive(n, 2, shift)
                for t in range(TB):
                    ts = slice(P * t, P * t + P)
                    for k in range(2):
                        for half in range(2):
                            cs = slice(BANK * half, BANK * half + BANK)
                            last = mm3(ps[:, bank0 + 2 * t + half, :], sh[:, k0 + k, ts], sl[:, k0 + k, ts],
                                       wh[:, k, cs], wl[:, k, cs], first and k == 0, last_k and k == 1)
                    if last_k and t == 0:
                        last.then_inc(rows_ps, 1)
                return last

            pe.wait_ge(sq_in, 16)
            norm_T(N_MIX0)
            pe.wait_ge(xT_done, 2)

            def w_in(n):
                pe.wait_ge(lo_done, n + 1)
                for m in range(2):
                    blk = 2 * n + m
                    if 4 <= blk < 12:
                        pe.wait_ge(xr_done, blk - 3)
                    elif blk >= 12:
                        pe.wait_ge(gelu_done, blk - 11)
                    last = transposed_product(n, m, ps[:, blk % 4, 0:S])
                    last.then_inc(pe_used if m else in_ps, 1)

            def gate_products(half):
                pe.wait_ge(bd_in, 64)
                for b in range(4 * half, 4 * half + 4):
                    pe.wait_ge(conv_done, b + 1)
                    if half:
                        pe.wait_ge(ri_ev, 2 * (b - 4) + 2)
                    for w in range(2):
                        last = mm(ps[:, 4 + b % 4, S * w:S * w + S], bd[:, w, b, :], xc[:, b, :], start=True, stop=True)
                    last.then_inc(ri_ps, 1)

            w_in(0)
            pe.wait_ge(par_in, 16 * 7)
            nc.tensor.transpose(ps[:, 4, 0:96], par_rows[:, :], ident[0:96, 0:96]).then_inc(setup_ps, 1)
            w_in(1)
            w_in(2)
            pe.wait_ge(prm_done, 1)
            gate_products(0)
            w_in(3)
            w_in(4)
            gate_products(1)
            for n in range(5, 8):
                w_in(n)
            pe.wait_ge(ri_ev, 2 * KD)
            pe.wait_ge(relb_in, 16)
            pe.wait_ge(relb_set, 1)
            pe.wait_ge(hot_in, 16)
            mm(ps[0:H, 4, :], relb[:, :], hotv[:, 0, :], start=True, stop=True).then_inc(setup_ps, 1)
            for b in range(TB):
                for c in range(NC):
                    at_ = P * b - CS * c - (CB - 1) + 256
                    o = (b * NC + c) * H
                    last = mm(ps[:, 5, o:o + H], hotv[:, 1, at_:at_ + P], relb[:, :], start=True, stop=True)
            last.then_inc(setup_ps, 1)
            for n in range(4):
                pe.wait_ge(yl_done, n // 2 + 1)
                rows_product(C_OUT + n, 2 * n, 0, xTh, xTl, n == 0, n == 3).then_inc(pe_used, 1)

            pe.wait_ge(setup_ev, 1)
            norm_T(N_FFN0)
            pe.wait_ge(xT_done, 2 * N_FFN0 + 2)

            def down(b, n):
                pe.wait_ge(fhl_done, b + 1)
                rows_product(n, 0, 0, fhh[:, b % 2], fhl[:, b % 2], b == 0, b == NFB - 1).then_inc(pe_used, 1)

            n = C_FFN
            for b in range(NFB):
                if b >= 2:
                    pe.wait_ge(fh_done, b - 1)
                for part in range(2):
                    pe.wait_ge(lo_done, n + 1)
                    for m in range(2):
                        last = transposed_product(n, m, ps[:, 4 + 2 * (b % 2) + m, S * part:S * part + S])
                    last.then_inc(pe_used, 1)
                    n += 1
                if b:
                    down(b - 1, n)
                    n += 1

            def p_T(k, bank):
                pe.wait_ge(p_in, 16 * k)
                for kk in range(2):
                    for t in range(TB):
                        last = nc.tensor.transpose(ps[:, bank, S * kk + P * t:S * kk + P * t + P],
                                                   pn[:, t, P * kk:P * kk + P], ident)
                last.then_inc(pT_ps, 1)

            p_T(1, 4)
            down(NFB - 1, n)
            pe.wait_ge(x_upd, U_PLE0)
            pe.wait_ge(pTl_done, 1)
            rows_product(C_PP0, 0, 0, pTh, pTl, True, True).then_inc(pe_used, 1)
            norm_T(N_PLE0)
            for n in range(4):
                if n == 0:
                    pe.wait_ge(xT_done, 2 * N_PLE0 + 2)
                rows_product(C_PG0 + n, 2 * n, 4, xTh, xTl, n == 0, n == 3).then_inc(pe_used, 1)
            norm_T(N_KV)
            pe.wait_ge(xT_done, 2 * N_KV + 2)

            def value_rows(n, bank):
                wh, wl = chunk_view(whi, n, KD), chunk_view(wlo, n, KD)
                for t in range(TB):
                    for k in range(KD):
                        ts = slice(P * t, P * t + P)
                        last = mm3(ps[:, bank, P * t:P * t + P], xTh[:, k, ts], xTl[:, k, ts],
                                   wh[:, k, P:2 * P], wl[:, k, P:2 * P], k == 0, k == KD - 1)
                return last

            pe.wait_ge(lo_done, C_KV + 1)
            transposed_product(C_KV, 0, ps[:, 0, 0:S])
            transposed_product(C_KV, 1, ps[:, 1, 0:S]).then_inc(pe_used, 1)
            pe.wait_ge(lo_done, C_KV + 2)
            transposed_product(C_KV + 1, 0, ps[:, 2, 0:S])
            value_rows(C_KV + 1, 3).then_inc(pe_used, 1)
            pe.wait_ge(lo_done, C_KV + 3)
            transposed_product(C_KV + 2, 0, ps[:, 6, 0:S])
            value_rows(C_KV + 2, 7).then_inc(pe_used, 1)
            pe.wait_ge(ml_done, 1)
            for w in range(2):
                for part in range(2):
                    n = C_W1 + 2 * w + part
                    wh, wl = arrive(n, 8)
                    for l in range(8):
                        last = mm3(ps[0:G * NC, 4 - 2 * w, 0:HID], mh[:, w, 8 * part + l, :], ml[:, w, 8 * part + l, :],
                                   wh[:, l, :], wl[:, l, :], part == 0 and l == 0, part == 1 and l == 7)
                    last.then_inc(pe_used, 1)
            pe.wait_ge(hidr_done, 2)
            for w in range(2):
                for k in range(2):
                    last = nc.tensor.transpose(ps[:, 5, 64 * w + 32 * k:64 * w + 32 * k + G * NC],
                                               hidr[:, w, P * k:P * k + P], ident[0:G * NC, 0:G * NC])
            last.then_inc(hid_ps, 1)
            pe.wait_ge(hid_done, 1)
            pe.wait_ge(w2_in, 32)
            for half in range(2):
                for k in range(2):
                    last = mm(ps[64 * half:64 * half + 64, 0, 0:G * NC], w2s[:, 0, k, :], hid[:, 0, k, :],
                              start=k == 0, stop=k == 1)
            last.then_inc(w2_ps, 1)
            for g in range(G):
                for k in range(2):
                    last = mm(ps[0:NC, 1, DH * g:DH * g + DH], hid[:, 1, k, NC * g:NC * g + NC], w2s[:, 1, k, :],
                              start=k == 0, stop=k == 1)
            last.then_inc(w2_ps, 1)
            norm_T(N_MIX1)
            pe.wait_ge(xT_done, 2 * N_MIX1 + 2)
            pe.wait_ge(kcd_done, 1)
            pe.wait_ge(vcb_done, 8)
            pe.wait_ge(kd_done, 10)
            for n in range(4):
                pe.wait_ge(lo_done, C_Q + n + 1)
                for m in range(2):
                    blk = 2 * n + m
                    if blk >= 4:
                        pe.wait_ge(q_ev, blk - 3)
                    transposed_product(C_Q + n, m, ps[:, blk % 4, 0:S]).then_inc(pe_used if m else q_ps, 1)
            wh, wl = arrive(C_QG, KD)
            for t in range(TB):
                ts = slice(P * t, P * t + P)
                for k in range(KD):
                    last = mm3(ps[:, 4, 48 * t:48 * t + 48], xTh[:, k, ts], xTl[:, k, ts], wh[:, k, :], wl[:, k, :],
                               k == 0, k == KD - 1)
            last.then_inc(pe_used, 1)
            pe.wait_ge(q_ev, KD)
            for b in range(TB):
                if b:
                    pe.wait_ge(sc_done, b)
                for h in range(H):
                    hp, par, g = h // 2, h % 2, h // 8
                    hs = slice(64 * par, 64 * par + 64)
                    last = mm(ps[:, par, NC * hp:NC * hp + NC], qT[hs, hp, P * b:P * b + P],
                              kcd[hs, NC * g:NC * g + NC], start=True, stop=True)
                last.then_inc(sc_ps, 1)
                pe.wait_ge(ec_done, b + 1)
                if b:
                    pe.wait_ge(ecT_done, b)
                for a in range(4):
                    last = nc.tensor.transpose(ps[:, 2, P * a:P * a + P],
                                               ec[:, 4 * a:4 * a + 4, :].rearrange("p a c -> p (a c)"), ident)
                last.then_inc(ecT_ps, 1)
                pe.wait_ge(ecT_done, b + 1)
                pe.wait_ge(gt_done, 1)
                for a in range(4):
                    o = S * (a % 2)
                    last = mm(ps[:, 4 + 2 * b + a // 2, o:o + S], ecT[:, a, :], vcb[:, a // 2, :], start=True, stop=True)
                last.then_inc(oc_ps, 1)

            def scores(n):
                b, h = divmod(n, H)
                hs = slice(64 * (h % 2), 64 * (h % 2) + 64)
                if n >= 2:
                    pe.wait_ge(S_done, n - 1)
                for br in range(2):
                    last = mm(ps[:, n % 2, S * br:S * br + P * (b + 1)], qT[hs, h // 2, P * b:P * b + P],
                              kd[hs, br, h // 8, 0:P * (b + 1)], start=True, stop=True)
                last.then_inc(S_ps, 1)

            def weighted(n):
                b, h = divmod(n, H)
                pe.wait_ge(PT_done, n + 1)
                if n == H:
                    pe.wait_ge(o_done, 1)
                for br in range(2):
                    for k in range(b + 1):
                        o = P * ((b + 1) * br + k)
                        last = mm(ps[:, 4 + 2 * br + h // 8, DH * (h % 8):DH * (h % 8) + DH], PTs[:, n % 2, o:o + P],
                                  vn[:, br, P * k + DH * (h // 8):P * k + DH * (h // 8) + DH],
                                  start=k == 0, stop=k == b)
                last.then_inc(pv_ps, 1)

            pe.wait_ge(sc_done, 2)
            pe.wait_ge(oc_ev, 4)
            scores(0)
            for n in range(TB * H):
                b = n // H
                if n + 1 < TB * H:
                    scores(n + 1)
                pe.wait_ge(P_done, n + 1)
                if n >= 2:
                    pe.wait_ge(PT_done, n - 1)
                for br in range(2):
                    for k in range(b + 1):
                        o = P * ((b + 1) * br + k)
                        last = nc.tensor.transpose(ps[:, 2 + n % 2, o:o + P], Psb[:, n % 2, br, P * k:P * k + P], ident)
                last.then_inc(PT_ps, 1)
                if n:
                    weighted(n - 1)
            weighted(TB * H - 1)
            for t in range(TB):
                pe.wait_ge(o_done, t + 1)
                pe.wait_ge(PT_done, TB * H)
                pe.wait_ge(S_done, TB * H)
                for k in range(KD):
                    last = nc.tensor.transpose(ps[:, 2 * t + k // 4, P * (k % 4):P * (k % 4) + P],
                                               oac[:, t, P * k:P * k + P], ident)
                last.then_inc(oT_ps, 1)
            pe.wait_ge(oT_done, 2)
            for n in range(4):
                rows_product(C_WO + n, 2 * n, 0, xTh, xTl, n == 0, n == 3).then_inc(pe_used, 1)
            norm_T(N_FFN1)
            pe.wait_ge(xT_done, 2 * N_FFN1 + 2)
            p_T(2, 2)
            wh, wl = arrive(C_RT, KD)
            for t in range(TB):
                ts = slice(P * t, P * t + P)
                for k in range(KD):
                    last = mm3(ps[:, 0, E * t:E * t + E], xTh[:, k, ts], xTl[:, k, ts], wh[:, k, :], wl[:, k, :],
                               k == 0, k == KD - 1)
            last.then_inc(pe_used, 1)
            pe.wait_ge(sel_done, 1)
            pe.wait_ge(relb_set, 2)
            mm(ps[:, 1, 0:E], before, sel[:, 0, :], start=True, stop=True)
            mm(ps[:, 1, E:2 * E], ones[:, :], sel[:, 0, :], start=True, stop=False)
            mm(ps[:, 1, E:2 * E], before, sel[:, 1, :], start=False, stop=True)
            mm(ps[:, 1, 2 * E:3 * E], ones[:, :], sel[:, 0, :], start=True, stop=False)
            mm(ps[:, 1, 2 * E:3 * E], ones[:, :], sel[:, 1, :], start=False, stop=True).then_inc(cnt_ps, 1)

            def gather(half):
                for c in range(4):
                    for t in range(TB):
                        o = P * (4 * half + c)
                        last = mm(ps[:, 7, P * c:P * c + P], xn[:, t, o:o + P], Pm[:, t, :], start=t == 0, stop=t == 1)
                last.then_inc(m_ps, 1)

            def scatter(k, bank=7):
                t, n = divmod(k, 2)
                mm(ps[:, bank, :], PmT[:, P * t:P * t + P], osb[:, BANK * n:BANK * (n + 1)], start=True, stop=True)\
                    .then_inc(m_ps, 1)

            pe.wait_ge(p_ready, 1)
            gather(0)
            pe.wait_ge(m_ev, 1)
            gather(1)
            pe.wait_ge(pTl_done, 2)
            pe.wait_ge(meta_done, 1)
            over = nc.tensor.value_load(metai[0:1, 0:1], min_val=0, max_val=3)
            with pe.Fori(0, over + E) as i:
                c0 = nc.tensor.snap(i * EC)
                i7 = nc.tensor.snap(i * 7)

                def gate_up(c, j, half):
                    for part in range(2):
                        wh, wl = arrive(C_MOE + c + part, 4, c0)
                        for k in range(4):
                            kk = 4 * half + k
                            last = mm3(ps[:, 2 * (j % 2) + part, :], xeh[:, kk, :], xel[:, kk, :], wh[:, k, :],
                                       wl[:, k, :], kk == 0, kk == KD - 1)
                        last.then_inc(pe_used, 1)

                def hidden_T(j):
                    pe.wait_ge(hm_done, i7 + (HM0 + j + 1))
                    pe.wait_ge(ht_done, i7 + (HT0 + j))
                    for f in range(4):
                        last = nc.tensor.transpose(ps[:, 4, P * f:P * f + P], hm[:, j % 2, P * f:P * f + P], ident)
                    last.then_inc(t_ps, 1)

                def down_rows(c, j):
                    pe.wait_ge(ht_done, i7 + (HT0 + j + 1))
                    if j == 0:
                        pe.wait_ge(osb_done, i + OS0)
                    for part in range(2):
                        wh, wl = arrive(C_MOE + c + part, 2, c0)
                        for k in range(2):
                            f = 2 * part + k
                            for n in range(2):
                                cs = slice(BANK * n, BANK * n + BANK)
                                last = mm3(ps[:, 5 + n, :], hth[:, f, :], htl[:, f, :], wh[:, k, cs], wl[:, k, cs],
                                           j == 0 and f == 0, j == NJ - 1 and f == 3)
                        last.then_inc(pe_used, 1)

                pe.wait_ge(m_ev, i7 + 2)
                c = 0
                for j in range(NJ):
                    pe.wait_ge(hm_done, i7 + (HM0 + j - 1))
                    gate_up(c, j, 0)
                    c += 2
                    if j < 2:
                        if j == 0:
                            pe.wait_ge(osb_done, i + OS0)
                        pe.wait_ge(m_ev, i7 + (2 + 2 * j))
                        scatter(2 * j)
                    if j:
                        hidden_T(j - 1)
                    if j == NJ - 1:
                        pe.wait_ge(p_ready, i + 2)
                        pe.wait_ge(m_ev, i7 + (2 + 5))
                        gather(0)
                    gate_up(c, j, 1)
                    c += 2
                    if j < 2:
                        pe.wait_ge(m_ev, i7 + (2 + 2 * j + 1))
                        scatter(2 * j + 1)
                    if j:
                        down_rows(c, j - 1)
                        c += 2
                    if j == 1:
                        pe.wait_ge(m_ev, i7 + (2 + 4))
                        for t in range(TB):
                            last = nc.tensor.transpose(ps[:, 7, P * t:P * t + P], Pm[:, t, :], ident)
                        last.then_inc(m_ps, 1)
                hidden_T(NJ - 1)
                pe.wait_ge(m_ev, i7 + (2 + 6))
                gather(1)
                down_rows(c, NJ - 1)
            n_item = nc.tensor.snap(over + E)
            c1 = nc.tensor.snap(n_item * EC)
            m0 = nc.tensor.snap(n_item * 7)
            pe.wait_ge(osb_done, n_item + OS0)
            pe.wait_ge(m_ev, m0 + 2)
            for k in range(4):
                scatter(k, 7 - k)
            pe.wait_ge(hm_done, m0 + HM0)

            rows_product(C_MOE, 0, 0, pTh, pTl, True, True, shift=c1).then_inc(pe_used, 1)
            pe.wait_ge(fin_scatter, 4)
            norm_T(N_PLE1)
            pe.wait_ge(xT_done, 2 * N_PLE1 + 2)
            for n in range(4):
                rows_product(C_MOE + 1 + n, 2 * n, 4, xTh, xTl, n == 0, n == 3, shift=c1).then_inc(pe_used, 1)


_INS = ['x', 'p', 'g_mix', 'g_ffn', 'g_ple', 'g_final', 'rg_w_in', 'rg_conv_w', 'rg_conv_b', 'rg_w_a', 'rg_b_a',
        'rg_w_x', 'rg_b_x', 'rg_lambda', 'rg_w_out', 'kv_norm', 'w_kv', 'cmp_pos_k', 'cmp_pos_v', 'cmp_k_w1',
        'cmp_k_w2', 'cmp_v_w1', 'cmp_v_w2', 'rel_bias', 'nsa_w_q', 'nsa_w_o', 'ffn_w_gu', 'ffn_w_down',
        'moe_w_router', 'moe_w_gu', 'moe_w_down', 'ple_w_proj', 'ple_w_gate']


def kernel(**inputs):
    import concourse.bacc as _bacc
    from concourse.bass_utils import run_bass_kernel_spmd as _run

    nc = _bacc.Bacc("TRN2", target_bir_lowering=False, num_devices=1)
    square, hot = shape_constants()
    arrays, args = {}, []
    for name in _INS + ['square', 'hot']:
        a = {'square': square, 'hot': hot}.get(name)
        a = np.ascontiguousarray(inputs[name] if a is None else a)
        arrays[f"in_{name}_dram"] = a
        args.append(nc.dram_tensor(f"in_{name}_dram", a.shape, mybir.dt.from_np(a.dtype), kind="ExternalInput").ap())
    res = nc.dram_tensor("out_dram", (1, S, D), F32, kind="ExternalOutput").ap()
    trunk(nc, *args, res)
    r = _run(nc, [arrays], core_ids=[0])
    return r.results[0]["out_dram"]
```

```python
import math
from contextlib import ExitStack

import numpy as np

import concourse.bass as bass
from concourse import mybir

F32 = mybir.dt.float32
F32R = mybir.dt.float32r
I32 = mybir.dt.int32
ALU = mybir.AluOpType
ACT = mybir.ActivationFunctionType
AX = mybir.AxisListType

P = 128
D = 1024
S = 256
TB = S // P
KD = D // P
EPS = 1e-6
BANK = 512
CH = 2048
RAW = 7
SPL = 3
CONV = 4
H, G, DH = 16, 2, 64
HID = 256
NC = 15
CB, CS = 32, 16
NB = 32
FF = 3072
NFB = FF // 256
E, FE = 8, 3584
NJ = FE // BANK
EC = 6 * NJ
NITEM = 13
NEG = -1e30


def rel_bucket(dist):
    n = np.maximum(dist, 0)
    big = 16 + (np.log(np.maximum(n, 1) / 16.0) / math.log(8.0) * 16 + 1e-9).astype(np.int64)
    return np.where(n < 16, n, np.minimum(big, NB - 1))


def shape_constants():
    square = np.zeros((P, 4, P), np.float32)
    square[:, 0] = np.eye(P)
    square[:, 1] = np.triu(np.ones((P, P)), 1)
    square[:, 2] = np.arange(P)[None, :]
    square[:, 3, 0:64] = np.tril(np.ones((8, 8)), -1).reshape(-1)
    square[:, 3, 64:72] = np.arange(8)
    hot = np.zeros((NB + 1, 2, 512), np.float32)
    for way, dist in enumerate((255 - np.arange(512), np.arange(512) - 256)):
        hot[rel_bucket(dist), way, np.arange(512)] = 1.0
        hot[NB, way] = np.where(dist < 0, NEG, 0.0)
    return square, hot


C_IN = 0
C_OUT = C_IN + 8
C_FFN = C_OUT + 4
C_PP0 = C_FFN + 3 * NFB
C_PG0 = C_PP0 + 1
C_KV = C_PG0 + 4
C_W1 = C_KV + 3
C_Q = C_W1 + 4
C_QG = C_Q + 4
C_WO = C_QG + 1
C_RT = C_WO + 4
C_MOE = C_RT + 1

R_OUT, R_DOWN, R_PP0, R_PG0, R_WO, R_PP1, R_PG1 = range(1, 8)

N_MIX0, N_FFN0, N_PLE0, N_KV, N_MIX1, N_FFN1, N_PLE1, N_FIN = range(8)


def trunk(nc, x, p, g_mix, g_ffn, g_ple, g_final, rg_w_in, rg_conv_w, rg_conv_b, rg_w_a, rg_b_a, rg_w_x,
          rg_b_x, rg_lambda, rg_w_out, kv_norm, w_kv, cmp_pos_k, cmp_pos_v, cmp_k_w1, cmp_k_w2, cmp_v_w1,
          cmp_v_w2, rel_bias, nsa_w_q, nsa_w_o, ffn_w_gu, ffn_w_down, moe_w_router, moe_w_gu, moe_w_down,
          ple_w_proj, ple_w_gate, square, hot, out, upto=99):
    ctx = ExitStack()
    with ctx:
        def sb(name, shape, dt=F32, where=ctx):
            return where.enter_context(nc.sbuf_tensor(name, shape, dt))

        def sem(name):
            return ctx.enter_context(nc.semaphore(name))

        raw = sb("raw", [P, RAW, CH])
        whi = sb("whi", [P, SPL, CH], F32R)
        wlo = sb("wlo", [P, SPL, CH], F32R)
        X = sb("X", [P, TB, D])
        xn = sb("xn", [P, TB, D])
        xTh = sb("xTh", [P, KD, S], F32R)
        xTl = sb("xTl", [P, KD, S], F32R)
        gain = sb("gain", [P, 2, D])
        sq = sb("sq", [P, 4, P])
        ident, before, iota = sq[:, 0, :], sq[:, 1, :], sq[:, 2, :]
        lower8 = sq[:, 3, 0:64].rearrange("p (j i) -> p j i", j=8)
        iota8 = sq[:, 3, 64:72]
        ones = sb("ones", [P, P])
        prm = sb("prm", [P, 96])
        cbias = sb("cbias", [P, TB, H, NC])
        cmask = sb("cmask", [P, TB, NC])
        ss = sb("ss", [P, TB])
        ms = sb("ms", [P, TB])
        std = sb("std", [P, TB])
        rstd = sb("rstd", [P, TB])
        spare = sb("spare", [P, 16])

        rg = ExitStack()
        par_rows = sb("par_rows", [96, P], where=rg)
        hotv = sb("hotv", [NB + 1, 2, 512], where=rg)
        relb = sb("relb", [NB + 1, H], where=rg)
        rev = sb("rev", [H, 512], where=rg)
        bd = sb("bd", [P, 2, KD, P], where=rg)
        xrp = sb("xrp", [P, KD, S + CONV - 1], where=rg)
        xc = sb("xc", [P, KD, S], where=rg)
        r_ = sb("r_", [P, 4, S], where=rg)
        i_ = sb("i_", [P, 4, S], where=rg)
        a_ = sb("a_", [P, 4, S], where=rg)
        s_ = sb("s_", [P, 4, S], where=rg)
        gg = sb("gg", [P, KD, S], where=rg)
        lsp = sb("lsp", [P, 6, KD], where=rg)
        rg.close()
        ff = ExitStack()
        pn = sb("pn", [P, TB, 256], where=ff)
        pTh = sb("pTh", [P, 2, S], F32R, where=ff)
        pTl = sb("pTl", [P, 2, S], F32R, where=ff)
        psg = sb("psg", [P, TB, D], where=ff)
        fsg = sb("fsg", [P, 2, 2, S], where=ff)
        fh = sb("fh", [P, 2, 2, S], where=ff)
        fhh = sb("fhh", [P, 2, 2, S], F32R, where=ff)
        fhl = sb("fhl", [P, 2, 2, S], F32R, where=ff)
        ff.close()
        at = ExitStack()
        tt = sb("tt", [P, H, S], where=at)
        kdh = sb("kdh", [P, 2, G, S], F32R, where=at)
        kdl = sb("kdl", [P, 2, G, S], F32R, where=at)
        vn = sb("vn", [P, 2, TB * P], where=at)
        kcd = sb("kcd", [P, G * NC], where=at)
        vcb = sb("vcb", [P, G, 4 * DH], where=at)
        qT = sb("qT", [P, KD, S], where=at)
        ov = qT[:, :, :].rearrange("p (r k c) s -> p r k (c s)", r=2, k=2)
        gt = sb("gt", [P, TB, 3 * H], where=at)
        qs = (xTh, xTl)
        oac = xn
        rs = sb("rs", [P, TB, 2, H], where=at)
        cf = sb("cf", [P, TB, 3, H], where=at)
        kv = ExitStack()
        kc2 = sb("kc2", [P, 2, G, S], where=kv)
        mf = sb("mf", [P, 2, CS, G, NC], where=kv)
        mh = sb("mh", [P, 2, CS, G * NC], F32R, where=kv)
        ml = sb("ml", [P, 2, CS, G * NC], F32R, where=kv)
        hid = sb("hid", [P, 2, 2, G * NC], where=kv)
        gtT = sb("gtT", [3 * H, S], where=kv)
        hidr = sb("hidr", [G * NC, 2, HID], where=kv)
        w2s = sb("w2s", [P, 2, 2, DH], where=kv)
        kv.close()
        sc = sb("sc", [P, H, NC], where=at)
        ec = sb("ec", [P, H, 32], where=at)
        ecT = sb("ecT", [P, 4, P], where=at)
        mxc = sb("mxc", [P, H], where=at)
        rsc = sb("rsc", [P, H], where=at)
        Ssb = sb("Ssb", [P, 2, 2, S], where=at)
        Psb = sb("Psb", [P, 2, 2, S], where=at)
        PTs = sb("PTs", [P, 2, BANK], where=at)
        nmx = sb("nmx", [P, 2, 2], where=at)
        at.close()
        mo = ExitStack()
        sb("embed_space", [P, 3 * 512 + TB * D], where=mo)
        xeh = sb("xeh", [P, KD, P], F32R, where=mo)
        xel = sb("xel", [P, KD, P], F32R, where=mo)
        Pm = sb("Pm", [P, TB, P], where=mo)
        PmT = sb("PmT", [P, S], where=mo)
        osb = sb("osb", [P, D], where=mo)
        msg = sb("msg", [P, BANK], where=mo)
        hm = sb("hm", [P, 2, BANK], where=mo)
        hth = sb("hth", [P, 4, P], F32R, where=mo)
        htl = sb("htl", [P, 4, P], F32R, where=mo)
        lgT = sb("lgT", [E, S], where=mo)
        lg = sb("lg", [P, TB, E], where=mo)
        cmpa = sb("cmpa", [P, TB, E, E], where=mo)
        cmpb = sb("cmpb", [P, TB, E, E], where=mo)
        sel = sb("sel", [P, TB, E], where=mo)
        rt = sb("rt", [P, 6, TB, E], where=mo)
        posit = sb("posit", [P, TB, NITEM], where=mo)
        combo = sb("combo", [P, TB, NITEM], where=mo)
        meta = sb("meta", [P, 4], where=mo)
        metai = sb("metai", [P, 4], I32, where=mo)
        mo.close()

        ps = ctx.enter_context(nc.psum_tensor("ps", [P, 8, BANK], F32))
        scratch = nc.dram_tensor("bias_by_distance", (H, P, 384), F32, kind="Internal").ap()

        raw_in = [sem(f"raw_in{n}") for n in range(RAW)]
        hi_done = sem("hi_done")
        lo_done = sem("lo_done")
        hi_half = sem("hi_half")
        lo_half = sem("lo_half")
        pe_used = sem("pe_used")
        x_in = [sem(f"x_in{t}") for t in range(TB)]
        sq_in = sem("sq_in")
        par_in = sem("par_in")
        hot_in = sem("hot_in")
        bd_zero = sem("bd_zero")
        bd_in = sem("bd_in")
        relb_set = sem("relb_set")
        relb_in = sem("relb_in")
        rev_out = sem("rev_out")
        tt_in = sem("tt_in")
        w2_in = sem("w2_in")
        p_in = sem("p_in")
        gain0_in = sem("gain0_in")
        gain_in = [sem(f"gain_in{n}") for n in range(2)]
        xrp_zero = sem("xrp_zero")
        setup_ps = sem("setup_ps")
        prm_done = sem("prm_done")
        rev_done = sem("rev_done")
        cb_ps = sem("cb_ps")
        exp_lam = sem("exp_lam")
        abs_lam = sem("abs_lam")
        sp_done = sem("sp_done")
        sumsq = sem("sumsq")
        meansq = sem("meansq")
        std_done = sem("std_done")
        xn_done = sem("xn_done")
        xT_ps = sem("xT_ps")
        xTh_done = sem("xTh_done")
        xT_done = sem("xT_done")
        x_upd = sem("x_upd")
        dve_own = sem("dve_own")
        in_ps = sem("in_ps")
        xr_done = sem("xr_done")
        conv_done = sem("conv_done")
        ri_ps = sem("ri_ps")
        ri_ev = sem("ri_ev")
        at_done = sem("at_done")
        m_done = sem("m_done")
        sqrt_done = sem("sqrt_done")
        gelu_done = sem("gelu_done")
        y_done = sem("y_done")
        yh_done = sem("yh_done")
        yl_done = sem("yl_done")
        fsg_done = sem("fsg_done")
        fh_done = sem("fh_done")
        fhh_done = sem("fhh_done")
        fhl_done = sem("fhl_done")
        pT_ps = sem("pT_ps")
        pTh_done = sem("pTh_done")
        pTl_done = sem("pTl_done")
        psg_done = sem("psg_done")
        ct_ev = sem("ct_ev")
        mf_done = sem("mf_done")
        mh_done = sem("mh_done")
        ml_done = sem("ml_done")
        kdh_done = sem("kdh_done")
        kd_done = sem("kd_done")
        qh_done = sem("qh_done")
        ql_done = sem("ql_done")
        hidr_done = sem("hidr_done")
        hid_ps = sem("hid_ps")
        hid_done = sem("hid_done")
        w2_ps = sem("w2_ps")
        kcd_done = sem("kcd_done")
        vcb_zero = sem("vcb_zero")
        vcb_done = sem("vcb_done")
        setup_ev = sem("setup_ev")
        fin_scatter = sem("fin_scatter")
        q_ps = sem("q_ps")
        q_ev = sem("q_ev")
        gtT_done = sem("gtT_done")
        gt_ps = sem("gt_ps")
        gt_done = sem("gt_done")
        sc_ps = sem("sc_ps")
        sc_done = sem("sc_done")
        ec_exp = sem("ec_exp")
        ec_done = sem("ec_done")
        ecT_ps = sem("ecT_ps")
        ecT_done = sem("ecT_done")
        oc_ps = sem("oc_ps")
        oc_ev = sem("oc_ev")
        S_ps = sem("S_ps")
        S_done = sem("S_done")
        nmx_done = sem("nmx_done")
        P_done = sem("P_done")
        PT_ps = sem("PT_ps")
        PT_done = sem("PT_done")
        pv_ps = sem("pv_ps")
        pv_ev = sem("pv_ev")
        o_done = sem("o_done")
        oT_ps = sem("oT_ps")
        oTh_done = sem("oTh_done")
        oT_done = sem("oT_done")
        lgT_done = sem("lgT_done")
        lg_ps = sem("lg_ps")
        lg_done = sem("lg_done")
        lge_done = sem("lge_done")
        sel_done = sem("sel_done")
        cnt_ps = sem("cnt_ps")
        meta_done = sem("meta_done")
        p_ready = sem("p_ready")
        rows_ps = sem("rows_ps")
        m_ps = sem("m_ps")
        m_ev = sem("m_ev")
        xeh_done = sem("xeh_done")
        xe_done = sem("xe_done")
        msg_done = sem("msg_done")
        hm_done = sem("hm_done")
        t_ps = sem("t_ps")
        hth_done = sem("hth_done")
        ht_done = sem("ht_done")
        osb_done = sem("osb_done")
        y_out = sem("y_out")
        fin_done = sem("fin_done")

        HM0, HT0, OS0 = 2, 1, 1
        U_FFN0, U_PLE0, U_KV, U_FFN1 = 4, 8, 10, 14

        def cols(w, a, n):
            return w[:, a:a + n].rearrange("(k p) n -> p k n", p=P)

        def rows(w, a, n):
            return w[a * P:(a + n) * P, :].rearrange("(k p) n -> p k n", p=P)

        w_in, w_out, w_q = rg_w_in[0], rg_w_out[0], nsa_w_q[0]
        gu0, dn0 = ffn_w_gu[0], ffn_w_down[0]
        static = [cols(w_in, D + 256 * n, 256) for n in range(4)]
        static += [cols(w_in, 256 * n, 256) for n in range(4)]
        static += [rows(w_out, 2 * n, 2) for n in range(4)]
        for b in range(NFB):
            static += [cols(gu0, 256 * b, 256), cols(gu0, FF + 256 * b, 256)]
            if b:
                static.append(rows(dn0, 2 * b - 2, 2))
        static.append(rows(dn0, 2 * NFB - 2, 2))
        static.append(rows(ple_w_proj[0], 0, 2))
        static += [rows(ple_w_gate[0], 2 * n, 2) for n in range(4)]
        static += [cols(w_kv, 256 * n, 256) for n in range(3)]
        for w1 in (cmp_k_w1, cmp_v_w1):
            static += [rows(w1, 8 * n, 8) for n in range(2)]
        static += [cols(w_q, 256 * n, 256) for n in range(4)]
        static.append(cols(w_q, D, 3 * H))
        static += [rows(nsa_w_o[0], 2 * n, 2) for n in range(4)]
        static.append(moe_w_router[0].rearrange("(k p) n -> p k n", p=P))
        assert len(static) == C_MOE
        size = [c.shape[1] * c.shape[2] for c in static]
        ple1 = [rows(ple_w_proj[1], 0, 2)] + [rows(ple_w_gate[1], 2 * n, 2) for n in range(4)]

        def expert_chunks(e):
            wg = moe_w_gu[0, bass.ds(e, 1), :, :].rearrange("a (k p) n -> p (a k) n", p=P)
            wd = moe_w_down[0, bass.ds(e, 1), :, :].rearrange("a (k p) n -> p (a k) n", p=P)
            order = []
            for j in range(NJ):
                for half in range(2):
                    for o in (0, FE):
                        order.append(wg[:, 4 * half:4 * half + 4, o + BANK * j:o + BANK * (j + 1)])
                if j:
                    order += [wd[:, 4 * j - 4 + 2 * n:4 * j - 2 + 2 * n, :] for n in range(2)]
            return order + [wd[:, 4 * NJ - 4 + 2 * n:4 * NJ - 2 + 2 * n, :] for n in range(2)]

        def chunk_view(t, n, k):
            width = size[n] if n < C_MOE else CH
            return t[:, n % SPL, 0:width].rearrange("p (k n) -> p k n", k=k)

        def wait_block(eng, first, chunk0, m):
            if m % 2 == 0:
                eng.wait_ge(first, m // 2 + 1)
            else:
                eng.wait_ge(pe_used, chunk0 + m // 2 + 1)

        def wait_rows(eng, k, last_chunk, t):
            if t == 0:
                eng.wait_ge(rows_ps, k)
            else:
                eng.wait_ge(pe_used, last_chunk + 1)

        def last_gu(b):
            return C_FFN + 3 * b + (1 if b == 0 else 0)

        block = ctx.enter_context(nc.Block())

        @block.sync
        def _(sp):
            for t in range(TB):
                sp.dma_start(X[:, t, :], x[0, P * t:P * t + P, :]).then_inc(x_in[t], 16)

            def load(n, src, shift=0):
                if n >= RAW:
                    sp.wait_ge(lo_done, shift + (n - RAW + 1))
                k, w = src.shape[1], src.shape[2]
                sp.dma_start(raw[:, n % RAW, 0:k * w].rearrange("p (k n) -> p k n", k=k), src)\
                    .then_inc(raw_in[n % RAW], 16)

            for n, src in enumerate(static):
                load(n, src)
                if n == 1:
                    sp.dma_start(par_rows[0:8 * CONV, :], rg_conv_w[0].rearrange("k (c p) -> (k c) p", p=P))\
                        .then_inc(par_in, 16)
                    for v, vec in enumerate((rg_conv_b[0], rg_b_a[0], rg_b_x[0], rg_lambda[0])):
                        to = 8 * (CONV + v)
                        sp.dma_start(par_rows[to:to + 8, :], vec.rearrange("(c p) -> c p", p=P)).then_inc(par_in, 16)
                    for v, pos in enumerate((cmp_pos_k, cmp_pos_v)):
                        sp.dma_start(par_rows[64 + 16 * v:80 + 16 * v, :].rearrange("l (a d) -> l a d", a=2),
                                     pos.rearrange("(l a) d -> l a d", a=2)).then_inc(par_in, 16)
                if n == 7:
                    sp.dma_start(hotv[:, :, :], hot).then_inc(hot_in, 16)
            with sp.Fori(0, E) as e:
                for c, src in enumerate(expert_chunks(e)):
                    load(C_MOE + c, src, e * EC)
            sp.wait_ge(meta_done, 1)
            over = nc.sync.value_load(metai[0:1, 0:1], min_val=0, max_val=3)
            with sp.If(over > 0):
                with sp.Fori(0, over) as k:
                    e = nc.sync.value_load(metai[0:1, bass.ds(k + 1, 1)], min_val=0, max_val=E - 1)
                    for c, src in enumerate(expert_chunks(e)):
                        load(C_MOE + c, src, k * EC + E * EC)
            for c, src in enumerate(ple1):
                load(C_MOE + c, src, over * EC + E * EC)
            for t in range(TB):
                sp.wait_ge(fin_done, t + 1)
                sp.dma_start(out[0, P * t:P * t + P, :], xn[:, t, :]).then_inc(y_out, 16)
            sp.wait_ge(y_out, 16 * TB)

        @block.gpsimd
        def _(pool):
            nc.gpsimd.memset(bd[:, :, :, :], 0.0).then_inc(bd_zero, 1)
            nc.gpsimd.memset(relb[:, :], 1.0).then_inc(relb_set, 1)
            nc.gpsimd.memset(xrp[:, :, 0:CONV - 1], 0.0).then_inc(xrp_zero, 1)
            nc.gpsimd.memset(ones[:, :], 1.0).then_inc(relb_set, 1)
            gains = [g_mix[0], g_ffn[0], g_ple[0], kv_norm, g_mix[1], g_ffn[1], g_ple[1], g_final]

            def load_gain(n):
                if n >= 2:
                    pool.wait_ge(xn_done, 2 * (n - 1))
                src = gains[n].rearrange("(a n) -> a n", a=1).broadcast_to([P, D])
                pool.dma_start(gain[:, n % 2, :], src).then_inc(gain_in[n % 2], 16)

            pool.wait_ge(bd_zero, 1)
            for w, src in enumerate((rg_w_a, rg_w_x)):
                by_par = src[0].rearrange("(b two) i o -> two i b o", two=2)
                for par in range(2):
                    h = slice(64 * par, 64 * par + 64)
                    pool.dma_start(bd[h, w, :, h], by_par[par]).then_inc(bd_in, 16)
            pool.wait_ge(relb_set, 1)
            pool.dma_start(relb[0:NB, :], rel_bias).then_inc(relb_in, 16)
            load_gain(1)
            pool.wait_ge(rev_done, 1)
            pool.dma_start(scratch, rev[:, 0:384].unsqueeze(1).broadcast_to([H, P, 384])).then_inc(rev_out, 16)
            pool.wait_ge(x_upd, U_FFN0)
            pool.dma_start(pn[:, :, :], p[0, 0].rearrange("(t p) n -> p t n", p=P)).then_inc(p_in, 16)
            load_gain(2)
            load_gain(3)
            pool.wait_ge(x_upd, U_KV)
            nc.gpsimd.memset(vcb[:, :, :], 0.0).then_inc(vcb_zero, 1)
            pool.wait_ge(rev_out, 16)
            pool.dma_start(tt[:, :, :], bass.AP(scratch.tensor, P - 1, [[383, P], [384 * P, H], [1, S]])).then_inc(tt_in, 16)
            for w, src in enumerate((cmp_k_w2, cmp_v_w2)):
                pool.dma_start(w2s[:, w, :, :], src.rearrange("(k p) n -> p k n", p=P)).then_inc(w2_in, 16)
            load_gain(4)
            load_gain(5)
            pool.wait_ge(x_upd, U_FFN1)
            pool.dma_start(pn[:, :, :], p[1, 0].rearrange("(t p) n -> p t n", p=P)).then_inc(p_in, 16)
            load_gain(6)
            load_gain(7)

        @block.scalar
        def _(act):
            act.dma_start(sq[:, :, :], square).then_inc(sq_in, 16)
            act.dma_start(gain[:, 0, :], g_mix[0].rearrange("(a n) -> a n", a=1).broadcast_to([P, D]))\
                .then_inc(gain0_in, 16)
            done = [0]

            def split_hi(n, width=CH, shift=0, uses=0):
                act.wait_ge(raw_in[n % RAW], 16 * (n // RAW + 1) + uses)
                if n >= SPL:
                    act.wait_ge(pe_used, shift + (n - SPL + 1))
                nc.scalar.activation(whi[:, n % SPL, 0:width], raw[:, n % RAW, 0:width], ACT.Copy)\
                    .then_inc(hi_done, 1)

            def half_hi(n, part):
                if part == 0:
                    act.wait_ge(raw_in[n % RAW], 16 * (n // RAW + 1))
                    act.wait_ge(pe_used, n - SPL + 1)
                cs = slice(CH // 2 * part, CH // 2 * (part + 1))
                last = nc.scalar.activation(whi[:, n % SPL, cs], raw[:, n % RAW, cs], ACT.Copy)
                last.then_inc(hi_done if part else hi_half, 1)
                done[0] += part

            def hi_to(n):
                while done[0] < n:
                    split_hi(done[0], size[done[0]] if done[0] < C_MOE else CH)
                    done[0] += 1

            warmed = [-1]

            def warm(function):
                warmed[0] += 1
                nc.scalar.activation(spare[:, warmed[0]:warmed[0] + 1], nc.const_aps.tensor(0.0, (P, 1), F32), function)

            def stats(n, sem_, counts):
                warm(ACT.Sqrt)
                for t in range(TB):
                    act.wait_ge(sem_[t], counts[t])
                    nc.scalar.activation(xn[:, t, :], X[:, t, :], ACT.Square, accum_out=ss[:, t:t + 1])\
                        .then_inc(sumsq, 1)
                    act.wait_ge(meansq, 2 * (n - 1) + t + 1)
                    nc.scalar.activation(std[:, t:t + 1], ms[:, t:t + 1], ACT.Sqrt).then_inc(std_done, 1)

            def xT_hi(n):
                for t in range(TB):
                    act.wait_ge(xT_ps, 2 * n + t + 1)
                    nc.scalar.activation(xTh[:, :, P * t:P * t + P],
                                         ps[:, 4 + 2 * t:6 + 2 * t, :].rearrange("p a (b n) -> p (a b) n", n=P),
                                         ACT.Copy).then_inc(xTh_done, 1)

            stats(1, x_in, (16, 16))
            hi_to(1)
            xT_hi(N_MIX0)
            hi_to(3)
            act.wait_ge(abs_lam, 1)
            nc.scalar.activation(lsp[:, 1, :], lsp[:, 0, :], ACT.Exp).then_inc(exp_lam, 1)

            def xr(m):
                wait_block(act, in_ps, C_IN, m)
                if m == 0:
                    act.wait_ge(xrp_zero, 1)
                nc.scalar.activation(xrp[:, m, CONV - 1:], ps[:, m % 4, 0:S], ACT.Copy).then_inc(xr_done, 1)

            def gates_of(half):
                if half:
                    act.wait_ge(y_done, 1)
                for b in range(4 * half, 4 * half + 4):
                    act.wait_ge(ri_ps, b + 1)
                    for dst, at_, v in ((r_, 0, 5), (i_, S, 6)):
                        nc.scalar.activation(dst[:, b % 4, :], ps[:, 4 + b % 4, at_:at_ + S], ACT.Sigmoid,
                                             bias=prm[:, 8 * v + b:8 * v + b + 1]).then_inc(ri_ev, 1)

            def decay_of(half):
                act.wait_ge(ri_ev, 8 * half + 8)
                act.wait_ge(sp_done, 2)
                for b in range(4 * half, 4 * half + 4):
                    nc.scalar.activation(a_[:, b % 4, :], r_[:, b % 4, :], ACT.Exp, scale=lsp[:, 5, b:b + 1])
                    last = nc.scalar.activation(s_[:, b % 4, :], r_[:, b % 4, :], ACT.Tanh, scale=lsp[:, 4, b:b + 1])
                    last.then_inc(at_done, 1)

            def root_of(half):
                act.wait_ge(m_done, half + 1)
                nc.scalar.activation(s_[:, :, :], s_[:, :, :], ACT.Sqrt).then_inc(sqrt_done, 1)

            def gelu(m):
                wait_block(act, in_ps, C_IN, KD + m)
                nc.scalar.activation(gg[:, m, :], ps[:, m % 4, 0:S], ACT.Gelu_apprx_tanh).then_inc(gelu_done, 1)

            act.wait_ge(prm_done, 1)
            for m in range(6):
                hi_to(C_IN + m // 2 + 4)
                xr(m)
            hi_to(6)
            gates_of(0)
            hi_to(7)
            xr(6)
            xr(7)
            decay_of(0)
            hi_to(8)
            gelu(0)
            gelu(1)
            root_of(0)
            hi_to(9)
            gelu(2)
            gelu(3)
            gates_of(1)
            decay_of(1)

            def y_hi(half):
                act.wait_ge(y_done, half + 1)
                act.wait_ge(pe_used, C_IN + 8)
                nc.scalar.activation(xTh[:, 4 * half:4 * half + 4, :], gg[:, 4 * half:4 * half + 4, :], ACT.Copy)\
                    .then_inc(yh_done, 1)

            y_hi(0)
            hi_to(10)
            for m in range(4, 8):
                gelu(m)
            root_of(1)
            hi_to(11)
            y_hi(1)
            hi_to(C_FFN + 2)
            stats(2, (x_upd, x_upd), (U_FFN0 - 2, U_FFN0))
            hi_to(C_FFN + 3)
            xT_hi(N_FFN0)

            def f_silu(b):
                act.wait_ge(pe_used, last_gu(b) + 1)
                nc.scalar.activation(fsg[:, b % 2, :, :], ps[:, 4 + 2 * (b % 2):6 + 2 * (b % 2), 0:S], ACT.Silu)\
                    .then_inc(fsg_done, 1)

            def f_hi(b):
                act.wait_ge(fh_done, b + 1)
                nc.scalar.activation(fhh[:, b % 2, :, :], fh[:, b % 2, :, :], ACT.Copy).then_inc(fhh_done, 1)

            act.wait_ge(rev_out, 16)
            for b in range(NFB):
                hi_to(last_gu(b) + 4)
                f_silu(b)
                f_hi(b)
            act.wait_ge(pT_ps, 1)
            nc.scalar.activation(pTh[:, :, :], ps[:, 4, :].rearrange("p (k s) -> p k s", k=2), ACT.Copy)\
                .then_inc(pTh_done, 1)
            stats(3, (x_upd, x_upd), (U_PLE0 - 2, U_PLE0))
            hi_to(C_PP0 + 2)
            xT_hi(N_PLE0)
            hi_to(C_PP0 + 4)

            def embed_gate(k, last_chunk):
                warm(ACT.Sigmoid)
                for t in range(TB):
                    wait_rows(act, k, last_chunk, t)
                    nc.scalar.activation(psg[:, t, :], ps[:, 4 + 2 * t:6 + 2 * t, :].rearrange("p a n -> p (a n)"),
                                         ACT.Sigmoid).then_inc(psg_done, 1)

            hi_to(C_PG0 + 6)
            embed_gate(R_PG0, C_PG0 + 3)
            stats(4, (x_upd, x_upd), (U_KV - 1, U_KV))
            hi_to(C_PG0 + 7)
            xT_hi(N_KV)
            act.wait_ge(pe_used, C_KV + 1)
            for g in range(G):
                src = ps[64 * g:64 * g + 64, 1, 0:S]
                nc.scalar.activation(kc2[0:64, 1, g, :], src, ACT.Copy).then_inc(ct_ev, 1)
                nc.scalar.activation(kc2[64:128, 1, g, 0:S - 1], src[:, 1:S], ACT.Copy).then_inc(ct_ev, 1)
            act.wait_ge(mf_done, 1)
            nc.scalar.activation(mh[:, :, :, :], mf[:, :, :, :, :].rearrange("p a l g c -> p a l (g c)"), ACT.Copy)\
                .then_inc(mh_done, 1)
            hi_to(C_W1 + 1)
            act.wait_ge(pe_used, C_KV + 2)
            for g in range(G):
                for half in range(2):
                    nc.scalar.activation(kdh[64 * half:64 * half + 64, 0, g, :], ps[64 * g:64 * g + 64, 2, 0:S],
                                         ACT.Copy).then_inc(kdh_done, 1)
            nc.scalar.activation(vn[:, 0, :], ps[:, 3, 0:S], ACT.Copy).then_inc(kd_done, 1)
            hi_to(C_W1 + 2)
            act.wait_ge(pe_used, C_KV + 3)
            for g in range(G):
                for half in range(2):
                    nc.scalar.activation(kdh[64 * half:64 * half + 64, 1, g, :], ps[64 * g:64 * g + 64, 6, 0:S],
                                         ACT.Copy).then_inc(kdh_done, 1)

            def units(w):
                act.wait_ge(pe_used, C_W1 + 2 * w + 2)
                nc.scalar.activation(hidr[:, w, :], ps[0:G * NC, w, 0:HID], ACT.Gelu_apprx_tanh)\
                    .then_inc(hidr_done, 1)

            hi_to(C_W1 + 3)
            hi_to(C_W1 + 4)
            units(0)
            xT_hi(N_MIX1)
            hi_to(C_W1 + 6)
            units(1)
            for m in range(KD):
                hi_to(C_Q + m // 2 + 3)
                wait_block(act, q_ps, C_Q, m)
                nc.scalar.activation(qT[:, m, :], ps[:, 4 + m % 4, 0:S], ACT.Copy, scale=DH ** -0.5).then_inc(q_ev, 1)
                if m == 1:
                    act.wait_ge(hid_ps, 1)
                    nc.scalar.activation(hid[:, :, :, :],
                                         ps[:, 2, 0:128].rearrange("p (w k c) -> p w k c", w=2, k=2)[:, :, :, 0:G * NC],
                                         ACT.Copy).then_inc(hid_done, 1)
                if m == 3:
                    act.wait_ge(w2_ps, 1)
                    nc.scalar.activation(kcd[:, :], ps[:, 0, 0:G * NC], ACT.Copy).then_inc(kcd_done, 1)
            act.wait_ge(pe_used, C_QG + 1)
            nc.scalar.activation(gtT[:, :], ps[0:3 * H, 5, 0:S], ACT.Sigmoid).then_inc(gtT_done, 1)
            for half in range(2):
                for par in range(2):
                    own = slice(64 * par, 64 * par + 64)
                    nc.scalar.activation(qs[par][own, 4 * half:4 * half + 4, :],
                                         qT[own, 4 * half:4 * half + 4, :], ACT.Copy).then_inc(qh_done, 1)
            act.wait_ge(gt_ps, 1)
            nc.scalar.activation(gt[:, :, :], ps[:, 5, 0:96].rearrange("p (t n) -> p t n", t=TB), ACT.Copy)\
                .then_inc(gt_done, 1)
            warm(ACT.Exp)
            for b in range(TB):
                act.wait_ge(sc_done, b + 1)
                if b:
                    act.wait_ge(ecT_ps, b)
                nc.scalar.activation(ec[:, :, 0:NC], sc[:, :, :], ACT.Exp).then_inc(ec_exp, 1)
                act.wait_ge(ecT_ps, b + 1)
                if b:
                    act.wait_ge(oc_ps, b)
                nc.scalar.activation(ecT[:, :, :], ps[:, 4 + b, :].rearrange("p (a n) -> p a n", n=P), ACT.Copy)\
                    .then_inc(ecT_done, 1)

            def probs_T(n):
                w = 2 * P * (n // H + 1)
                act.wait_ge(PT_ps, n + 1)
                if n >= 2:
                    act.wait_ge(pv_ps, n - 1)
                nc.scalar.activation(PTs[:, n % 2, 0:w], ps[:, 2 + n % 2, 0:w], ACT.Copy).then_inc(PT_done, 1)

            for n in range(TB * H):
                b, h = divmod(n, H)
                w = P * (b + 1)
                act.wait_ge(nmx_done, n + 1)
                if n >= 2:
                    act.wait_ge(PT_ps, n - 1)
                for br in range(2):
                    last = nc.scalar.activation(Psb[:, n % 2, br, 0:w], Ssb[:, n % 2, br, 0:w], ACT.Exp,
                                                bias=nmx[:, n % 2, br:br + 1], accum_out=rs[:, b, br, h:h + 1])
                last.then_inc(P_done, 1)
                if n:
                    probs_T(n - 1)
                if n == H:
                    act.wait_ge(pv_ps, H)
                    nc.scalar.activation(ov[:, 1, :, :], ps[:, 6:8, :], ACT.Copy).then_inc(pv_ev, 1)
                if H + 6 <= n < H + 10:
                    half_hi(C_WO + 1 + (n - H - 6) // 2, n % 2)
            probs_T(TB * H - 1)
            for t in range(TB):
                act.wait_ge(oT_ps, t + 1)
                nc.scalar.activation(xTh[:, :, P * t:P * t + P],
                                     ps[:, 2 * t:2 * t + 2, :].rearrange("p a (b n) -> p (a b) n", n=P),
                                     ACT.Copy).then_inc(oTh_done, 1)
            hi_to(C_RT + 2)
            stats(5, (x_upd, x_upd), (U_FFN1 - 2, U_FFN1))
            hi_to(C_MOE + 2)
            xT_hi(N_FFN1)
            warm(ACT.Exp)
            act.wait_ge(lg_done, 1)
            nc.scalar.activation(rt[:, 0, :, :], rt[:, 0, :, :], ACT.Exp).then_inc(lge_done, 1)
            act.wait_ge(pT_ps, 2)
            nc.scalar.activation(pTh[:, :, :], ps[:, 2, :].rearrange("p (k s) -> p k s", k=2), ACT.Copy)\
                .then_inc(pTh_done, 1)
            hi_to(C_MOE + 3)
            for half in range(2):
                act.wait_ge(m_ps, half + 1)
                nc.scalar.activation(xeh[:, 4 * half:4 * half + 4, :],
                                     ps[:, 7 - half, :].rearrange("p (a n) -> p a n", n=P), ACT.Copy)\
                    .then_inc(xeh_done, 1)
            act.wait_ge(meta_done, 1)
            over = nc.scalar.value_load(metai[0:1, 0:1], min_val=0, max_val=3)
            with act.Fori(0, over + E) as i:
                c0 = nc.scalar.snap(i * EC)
                uses = nc.scalar.snap(i * (16 * EC // RAW))
                i7 = nc.scalar.snap(i * 7)

                def gathered(half):
                    act.wait_ge(m_ps, i7 + (2 + 5 + half + 1))
                    act.wait_ge(pe_used, c0 + (C_MOE + 6 * NJ - 4))
                    nc.scalar.activation(xeh[:, 4 * half:4 * half + 4, :],
                                         ps[:, 7, :].rearrange("p (a n) -> p a n", n=P), ACT.Copy)\
                        .then_inc(xeh_done, 1)

                def hidden_T(j):
                    act.wait_ge(t_ps, i7 + (j + 1))
                    if j:
                        act.wait_ge(pe_used, c0 + (C_MOE + 6 * j + 4))
                    nc.scalar.activation(hth[:, :, :], ps[:, 4, :].rearrange("p (a n) -> p a n", n=P), ACT.Copy)\
                        .then_inc(hth_done, 1)

                for c in range(EC):
                    if c == EC - 3:
                        hidden_T(NJ - 1)
                        gathered(1)
                    split_hi(C_MOE + c + 3, shift=c0, uses=uses)
                    if c == 3 or (c > 3 and c % 6 == 1):
                        j = 0 if c == 3 else c // 6
                        act.wait_ge(hm_done, i7 + (HM0 + j))
                        nc.scalar.activation(msg[:, :], ps[:, 2 * (j % 2), :], ACT.Silu).then_inc(msg_done, 1)
                    if c % 6 == 5 and c // 6 < NJ - 1:
                        hidden_T(c // 6)
                    if c == 6 * NJ - 5:
                        gathered(0)
                act.wait_ge(pe_used, c0 + (C_MOE + EC))
                nc.scalar.activation(osb[:, :], ps[:, 5:7, :].rearrange("p a n -> p (a n)"), ACT.Copy)\
                    .then_inc(osb_done, 1)
            n_item = nc.scalar.snap(over + E)
            c1 = nc.scalar.snap(n_item * EC)
            uses1 = nc.scalar.snap(n_item * (16 * EC // RAW))
            stats(6, (fin_scatter, fin_scatter), (2, 4))
            xT_hi(N_PLE1)
            split_hi(C_MOE + 3, shift=c1, uses=uses1)
            split_hi(C_MOE + 4, shift=c1, uses=uses1)
            embed_gate(R_PG1, c1 + (C_MOE + 4))
            stats(7, (x_upd, x_upd), (U_FFN1 + 1, U_FFN1 + 2))

        @block.vector
        def _(dve):
            v = nc.vector
            own, done = [0], [0]

            def link(ins):
                own[0] += 1
                ins.then_inc(dve_own, 1)
                dve.wait_ge(dve_own, own[0])

            def split_lo(n, width=CH, shift=0):
                dve.wait_ge(hi_done, shift + (n + 1))
                v.tensor_tensor(wlo[:, n % SPL, 0:width], raw[:, n % RAW, 0:width],
                                whi[:, n % SPL, 0:width].bitcast(F32), ALU.subtract).then_inc(lo_done, 1)

            def half_lo(n, part):
                if part:
                    dve.wait_ge(hi_done, n + 1)
                else:
                    dve.wait_ge(hi_half, n - C_WO)
                cs = slice(CH // 2 * part, CH // 2 * (part + 1))
                last = v.tensor_tensor(wlo[:, n % SPL, cs], raw[:, n % RAW, cs], whi[:, n % SPL, cs].bitcast(F32),
                                       ALU.subtract)
                last.then_inc(lo_done if part else lo_half, 1)
                done[0] += part

            def lo_to(n):
                while done[0] < n:
                    split_lo(done[0], size[done[0]] if done[0] < C_MOE else CH)
                    done[0] += 1

            def norm_stats(k, t):
                dve.wait_ge(sumsq, 2 * (k - 1) + t + 1)
                v.tensor_scalar(ms[:, t:t + 1], ss[:, t:t + 1], 1.0 / D, EPS, ALU.mult, ALU.add).then_inc(meansq, 1)
                dve.wait_ge(std_done, 2 * (k - 1) + t + 1)
                link(v.reciprocal(rstd[:, t:t + 1], std[:, t:t + 1]))

            def norm_rows(n, signal, k=None):
                for t in range(TB):
                    if k:
                        norm_stats(k, t)
                    if n:
                        dve.wait_ge(gain_in[n % 2], 16 * ((n + 1) // 2))
                    else:
                        dve.wait_ge(gain0_in, 16)
                    v.scalar_tensor_tensor(xn[:, t, :], X[:, t, :], rstd[:, t:t + 1], gain[:, n % 2, :],
                                           ALU.mult, ALU.mult).then_inc(signal, 1)

            def xT_lo(n):
                for t in range(TB):
                    dve.wait_ge(xTh_done, 2 * n + t + 1)
                    v.tensor_tensor(xTl[:, :, P * t:P * t + P],
                                    ps[:, 4 + 2 * t:6 + 2 * t, :].rearrange("p a (b n) -> p (a b) n", n=P),
                                    xTh[:, :, P * t:P * t + P].bitcast(F32), ALU.subtract).then_inc(xT_done, 1)

            def add_block(k, last_chunk):
                for t in range(TB):
                    wait_rows(dve, k, last_chunk, t)
                    for n in range(2):
                        to = X[:, t, BANK * n:BANK * (n + 1)]
                        v.tensor_tensor(to, ps[:, 2 * t + n, :], to, ALU.add).then_inc(x_upd, 1)

            norm_rows(N_MIX0, xn_done, 1)
            lo_to(1)
            xT_lo(N_MIX0)
            lo_to(3)
            dve.wait_ge(setup_ps, 1)
            v.tensor_copy(prm[:, :], ps[:, 4, 0:96]).then_inc(prm_done, 1)
            dve.wait_ge(prm_done, 1)
            lam = prm[:, 56:64]
            v.scalar_tensor_tensor(lsp[:, 0, :], lam, -1.0, lam, ALU.mult, ALU.min).then_inc(abs_lam, 1)
            dve.wait_ge(exp_lam, 1)
            y, z, z2, q = (lsp[:, n, :] for n in (1, 2, 3, 4))
            link(v.tensor_scalar(z, y, 2.0, None, ALU.add))
            link(v.reciprocal(z, z))
            link(v.tensor_tensor(z, y, z, ALU.mult))
            link(v.tensor_tensor(z2, z, z, ALU.mult))
            link(v.tensor_scalar(q, z2, 1.0 / 17, None, ALU.mult))
            for k in (15, 13, 11, 9, 7, 5, 3):
                link(v.scalar_tensor_tensor(q, q, 1.0 / k, z2, ALU.add, ALU.mult))
            link(v.scalar_tensor_tensor(q, q, 1.0, z, ALU.add, ALU.mult))
            link(v.tensor_scalar(lsp[:, 0, :], lam, -1.0, 0.0, ALU.mult, ALU.max))
            link(v.scalar_tensor_tensor(q, q, 2.0, lsp[:, 0, :], ALU.mult, ALU.add))
            v.tensor_scalar(lsp[:, 5, :], q, -8.0, None, ALU.mult).then_inc(sp_done, 1)
            dve.wait_ge(sp_done, 1)
            v.tensor_scalar(lsp[:, 4, :], q, 8.0, None, ALU.mult).then_inc(sp_done, 1)

            def conv(m):
                dve.wait_ge(xr_done, m + 1)
                link(v.tensor_scalar(xc[:, m, :], xrp[:, m, 0:S], prm[:, m:m + 1], prm[:, 32 + m:33 + m],
                                     ALU.mult, ALU.add))
                for k in range(1, CONV):
                    last = v.scalar_tensor_tensor(xc[:, m, :], xrp[:, m, k:k + S], prm[:, 8 * k + m:8 * k + m + 1],
                                                  xc[:, m, :], ALU.mult, ALU.add)
                    if k < CONV - 1:
                        link(last)
                last.then_inc(conv_done, 1)

            def y_lo(half):
                hs = slice(4 * half, 4 * half + 4)
                dve.wait_ge(yh_done, half + 1)
                v.tensor_tensor(xTl[:, hs, :], gg[:, hs, :], xTh[:, hs, :].bitcast(F32), ALU.subtract)\
                    .then_inc(yl_done, 1)

            def recur(half):
                hs = slice(4 * half, 4 * half + 4)
                dve.wait_ge(at_done, 4 * half + 4)
                link(v.tensor_tensor(r_[:, :, :], a_[:, :, :], a_[:, :, :], ALU.mult))
                v.scalar_tensor_tensor(s_[:, :, :], r_[:, :, :], 1.0, s_[:, :, :], ALU.add, ALU.mult).then_inc(m_done, 1)
                link(v.tensor_tensor(i_[:, :, :], i_[:, :, :], xc[:, hs, :], ALU.mult))
                if half:
                    y_lo(0)
                dve.wait_ge(sqrt_done, half + 1)
                link(v.tensor_tensor(i_[:, :, :], s_[:, :, :], i_[:, :, :], ALU.mult))
                for b in range(4):
                    last = v.tensor_tensor_scan(r_[:, b, :], a_[:, b, :], i_[:, b, :], 0.0, ALU.mult, ALU.add)
                link(last)
                if half == 0:
                    lo_to(9)
                dve.wait_ge(gelu_done, 4 * half + 4)
                v.tensor_tensor(gg[:, hs, :], gg[:, hs, :], r_[:, :, :], ALU.mult).then_inc(y_done, 1)

            for m in range(8):
                lo_to(C_IN + m // 2 + 4)
                conv(m)
            lo_to(8)
            recur(0)
            recur(1)
            lo_to(10)
            y_lo(1)
            lo_to(11)
            dve.wait_ge(setup_ps, 2)
            v.tensor_copy(rev[:, :], ps[0:H, 4, :]).then_inc(rev_done, 1)
            dve.wait_ge(setup_ps, 3)
            link(v.tensor_copy(cbias[:, :, :, :],
                               ps[:, 5, 0:TB * NC * H].rearrange("p (b c h) -> p b h c", b=TB, c=NC)))
            v.tensor_scalar(cmask[:, :, :], cbias[:, :, 0, :], NEG / 10, None, ALU.is_gt).then_inc(setup_ev, 1)
            lo_to(C_FFN + 2)
            add_block(R_OUT, C_OUT + 3)
            norm_rows(N_FFN0, xn_done, 2)
            xT_lo(N_FFN0)
            lo_to(C_FFN + 3)

            def f_mul(b):
                dve.wait_ge(fsg_done, b + 1)
                v.tensor_tensor(fh[:, b % 2, :, :], ps[:, 4 + 2 * (b % 2):6 + 2 * (b % 2), S:2 * S],
                                fsg[:, b % 2, :, :], ALU.mult).then_inc(fh_done, 1)

            def f_lo(b):
                dve.wait_ge(fhh_done, b + 1)
                v.tensor_tensor(fhl[:, b % 2, :, :], fh[:, b % 2, :, :], fhh[:, b % 2, :, :].bitcast(F32),
                                ALU.subtract).then_inc(fhl_done, 1)

            for b in range(NFB):
                lo_to(last_gu(b) + 4)
                f_mul(b)
                f_lo(b)

            def p_lo(k, bank):
                dve.wait_ge(pTh_done, k)
                v.tensor_tensor(pTl[:, :, :], ps[:, bank, :].rearrange("p (k s) -> p k s", k=2),
                                pTh[:, :, :].bitcast(F32), ALU.subtract).then_inc(pTl_done, 1)

            def embed(k):
                for t in range(TB):
                    dve.wait_ge(psg_done, TB * (k - 1) + t + 1)
                    link(v.tensor_tensor(psg[:, t, :], ps[:, 2 * t:2 * t + 2, :].rearrange("p a n -> p (a n)"),
                                         psg[:, t, :], ALU.mult))
                    v.tensor_tensor(X[:, t, :], psg[:, t, :], X[:, t, :], ALU.add).then_inc(x_upd, 1)

            p_lo(1, 4)
            lo_to(C_PP0 + 1)
            add_block(R_DOWN, C_PP0 - 1)
            norm_rows(N_PLE0, xn_done, 3)
            lo_to(C_PP0 + 2)
            xT_lo(N_PLE0)
            lo_to(C_PP0 + 4)
            lo_to(C_PG0 + 6)
            embed(1)
            norm_rows(N_KV, xn_done, 4)
            xT_lo(N_KV)
            lo_to(C_PG0 + 7)
            dve.wait_ge(pe_used, C_KV + 1)
            for g in range(G):
                src = ps[64 * g:64 * g + 64, 0, 0:S]
                v.tensor_copy(kc2[0:64, 0, g, :], src).then_inc(ct_ev, 1)
                v.tensor_copy(kc2[64:128, 0, g, 0:S - 1], src[:, 1:S]).then_inc(ct_ev, 1)
            dve.wait_ge(ct_ev, 8)
            for w in range(2):
                view = bass.AP(kc2, w * G * S, [[2 * G * S, P], [2, CS], [S, G], [CS, NC]])
                pos = prm[:, 64 + CS * w:64 + CS * (w + 1)]
                pos = bass.AP(pos.tensor, pos.offset, [list(pos.ap[0]), [1, CS], [0, G], [0, NC]])
                last = v.tensor_tensor(mf[:, w, :, :, :], view, pos, ALU.add)
            last.then_inc(mf_done, 1)
            dve.wait_ge(mh_done, 1)
            v.tensor_tensor(ml[:, :, :, :], mf[:, :, :, :, :].rearrange("p a l g c -> p a l (g c)"),
                            mh[:, :, :, :].bitcast(F32), ALU.subtract).then_inc(ml_done, 1)
            lo_to(C_W1 + 1)
            for br in range(2):
                dve.wait_ge(kdh_done, 4 * br + 4)
                for g in range(G):
                    for half in range(2):
                        hs = slice(64 * half, 64 * half + 64)
                        v.tensor_tensor(kdl[hs, br, g, :], ps[64 * g:64 * g + 64, 2 + 4 * br, 0:S],
                                        kdh[64 * g:64 * g + 64, br, g, :].bitcast(F32), ALU.subtract)\
                            .then_inc(kd_done, 1)
                if br == 0:
                    lo_to(C_W1 + 2)
                    norm_rows(N_MIX1, xn_done)
            dve.wait_ge(pe_used, C_KV + 3)
            v.tensor_copy(vn[:, 1, :], ps[:, 7, 0:S]).then_inc(kd_done, 1)
            lo_to(C_W1 + 4)
            xT_lo(N_MIX1)
            lo_to(C_Q + 4)
            dve.wait_ge(w2_ps, 2)
            dve.wait_ge(vcb_zero, 1)
            for g in range(G):
                for a in range(4):
                    v.tensor_copy(vcb[32 * a:32 * a + NC, g, DH * a:DH * (a + 1)],
                                  ps[0:NC, 1, DH * g:DH * (g + 1)]).then_inc(vcb_done, 1)
            lo_to(C_QG + 2)
            for half in range(2):
                hs = slice(4 * half, 4 * half + 4)
                for par in range(2):
                    dve.wait_ge(qh_done, 2 * half + par + 1)
                    mine, other = slice(64 * par, 64 * par + 64), slice(64 - 64 * par, 128 - 64 * par)
                    v.tensor_tensor(qs[par][other, hs, :], qT[mine, hs, :], qs[par][mine, hs, :].bitcast(F32),
                                    ALU.subtract).then_inc(ql_done, 1)

            v.memset(ec[:, :, :], 0.0)

            def by_head(a, width):
                return a.unsqueeze(2).broadcast_to([P, a.shape[1], width])

            def compressed_softmax(b):
                dve.wait_ge(sc_ps, b + 1)
                for par in range(2):
                    view = sc[:, :, :].rearrange("p (a two) c -> p a two c", two=2)[:, :, par, :]
                    bias = cbias[:, b, :, :].rearrange("p (a two) c -> p a two c", two=2)[:, :, par, :]
                    link(v.tensor_tensor(view, ps[:, 2 * b + par, 0:8 * NC].rearrange("p (a c) -> p a c", c=NC), bias, ALU.add))
                link(v.tensor_reduce(mxc[:, :], sc[:, :, :], AX.X, ALU.max))
                v.tensor_tensor(sc[:, :, :], sc[:, :, :], by_head(mxc[:, :], NC), ALU.subtract).then_inc(sc_done, 1)
                dve.wait_ge(ec_exp, b + 1)
                keep = cmask[:, b, :].unsqueeze(1).broadcast_to([P, H, NC])
                v.tensor_tensor(ec[:, :, 0:NC], ec[:, :, 0:NC], keep, ALU.mult).then_inc(ec_done, 1)
                dve.wait_ge(ec_done, b + 1)
                link(v.tensor_reduce(rsc[:, :], ec[:, :, 0:NC], AX.X, ALU.add))
                link(v.tensor_scalar(rsc[:, :], rsc[:, :], 1e-30, None, ALU.max))
                link(v.reciprocal(rsc[:, :], rsc[:, :]))
                dve.wait_ge(gt_done, 1)
                link(v.tensor_tensor(cf[:, b, 0, :], rsc[:, :], gt[:, b, 0:H], ALU.mult))

            def compressed_out(b):
                dve.wait_ge(oc_ps, b + 1)
                for n in range(2):
                    v.tensor_tensor(oac[:, b, BANK * n:BANK * (n + 1)].rearrange("p (h d) -> p h d", d=DH),
                                    ps[:, 6 - 2 * b + n, :].rearrange("p (h d) -> p h d", d=DH),
                                    by_head(cf[:, b, 0, 8 * n:8 * n + 8], DH), ALU.mult).then_inc(oc_ev, 1)

            compressed_softmax(0)
            compressed_out(0)
            compressed_softmax(1)

            def coefficients(b):
                dve.wait_ge(P_done, H * (b + 1))
                link(v.reciprocal(cf[:, b, 1:3, :], rs[:, b, :, :]))
                link(v.tensor_tensor(cf[:, b, 1:3, :], cf[:, b, 1:3, :],
                                     gt[:, b, H:3 * H].rearrange("p (a h) -> p a h", a=2), ALU.mult))

            def combine(b, br, k, src):
                link(v.tensor_tensor(ov[:, br, k, :].rearrange("p (h d) -> p h d", d=DH),
                                     src.rearrange("p (h d) -> p h d", d=DH),
                                     by_head(cf[:, b, 1 + br, 8 * k:8 * k + 8], DH), ALU.mult))
                to = oac[:, b, BANK * k:BANK * (k + 1)]
                o_count[0] += 1
                v.tensor_tensor(to, ov[:, br, k, :], to, ALU.add).then_inc(o_done, 1)
                dve.wait_ge(o_done, o_count[0])

            o_count = [0]

            dve.wait_ge(tt_in, 16)
            for n in range(TB * H):
                b, h = divmod(n, H)
                w = P * (b + 1)
                dve.wait_ge(S_ps, n + 1)
                if n >= 2:
                    dve.wait_ge(P_done, n - 1)
                bias = tt[:, h, S - w:S].unsqueeze(1).broadcast_to([P, 2, w])
                v.tensor_tensor(Ssb[:, n % 2, :, 0:w],
                                ps[:, n % 2, :].rearrange("p (r s) -> p r s", r=2)[:, :, 0:w],
                                bias, ALU.add).then_inc(S_done, 1)
                dve.wait_ge(S_done, n + 1)
                v.tensor_reduce(nmx[:, n % 2, :], Ssb[:, n % 2, :, 0:w], AX.X, ALU.max, negate=True)\
                    .then_inc(nmx_done, 1)
                if n == 1:
                    compressed_out(1)
                if n == H:
                    dve.wait_ge(pv_ps, H)
                    v.tensor_copy(ov[:, 0, :, :], ps[:, 4:6, :]).then_inc(pv_ev, 1)
                    coefficients(0)
                if H + 8 <= n < H + 12:
                    half_lo(C_WO + 1 + (n - H - 8) // 2, n % 2)
                if n in (H + 2, H + 3, H + 4, H + 5):
                    dve.wait_ge(pv_ev, 2)
                    br, k = divmod(n - H - 2, 2)
                    combine(0, br, k, ov[:, br, k, :])
            coefficients(1)
            dve.wait_ge(pv_ps, TB * H)
            for k in range(2):
                for br in range(2):
                    combine(1, br, k, ps[:, 4 + 2 * br + k, :])
            for t in range(TB):
                dve.wait_ge(oTh_done, t + 1)
                v.tensor_tensor(xTl[:, :, P * t:P * t + P],
                                ps[:, 2 * t:2 * t + 2, :].rearrange("p a (b n) -> p (a b) n", n=P),
                                xTh[:, :, P * t:P * t + P].bitcast(F32), ALU.subtract).then_inc(oT_done, 1)
            lo_to(C_RT + 1)
            v.memset(posit[:, :, :], -1.0)
            link(v.memset(combo[:, :, :], 0.0))
            v.memset(osb[:, :], 0.0).then_inc(osb_done, OS0)
            v.memset(PmT[:, :], 0.0).then_inc(ht_done, HT0)
            v.memset(hm[:, :, :], 0.0).then_inc(hm_done, HM0)
            lo_to(C_RT + 2)
            add_block(R_WO, C_WO + 3)
            norm_rows(N_FFN1, xn_done, 5)
            xT_lo(N_FFN1)
            lo_to(C_MOE + 2)
            dve.wait_ge(pe_used, C_RT + 1)
            v.tensor_copy(lgT[:, :], ps[0:E, 0, 0:S]).then_inc(lgT_done, 1)
            dve.wait_ge(lg_ps, 1)
            link(v.tensor_copy(lg[:, :, :], ps[:, 0, 0:TB * E].rearrange("p (t e) -> p t e", t=TB)))
            top, total = rt[:, 5, 0, 0:TB], rt[:, 5, 1, 0:TB]
            link(v.tensor_reduce(top, lg[:, :, :], AX.X, ALU.max))
            v.tensor_tensor(rt[:, 0, :, :], lg[:, :, :], top.unsqueeze(2).broadcast_to([P, TB, E]), ALU.subtract)\
                .then_inc(lg_done, 1)
            rank = rt[:, 1, :, :]
            for t in range(TB):
                li = lg[:, t, :].unsqueeze(1).broadcast_to([P, E, E])
                lj = lg[:, t, :].unsqueeze(2).broadcast_to([P, E, E])
                link(v.tensor_tensor(cmpa[:, t, :, :], li, lj, ALU.is_gt))
                link(v.tensor_tensor(cmpb[:, t, :, :], li, lj, ALU.is_equal))
                link(v.tensor_tensor(cmpb[:, t, :, :], cmpb[:, t, :, :], lower8, ALU.mult))
                link(v.tensor_tensor(cmpa[:, t, :, :], cmpa[:, t, :, :], cmpb[:, t, :, :], ALU.add))
            link(v.tensor_reduce(rank, cmpa[:, :, :, :], AX.X, ALU.add))
            v.tensor_scalar(sel[:, :, :], rank, 2.0, None, ALU.is_lt).then_inc(sel_done, 1)
            dve.wait_ge(sel_done, 1)
            dve.wait_ge(lge_done, 1)
            comb = rt[:, 2, :, :]
            link(v.tensor_tensor(comb, rt[:, 0, :, :], sel[:, :, :], ALU.mult))
            link(v.tensor_reduce(total, comb, AX.X, ALU.add))
            link(v.reciprocal(total, total))
            link(v.tensor_tensor(comb, comb, total.unsqueeze(2).broadcast_to([P, TB, E]), ALU.mult))
            link(v.tensor_copy(combo[:, :, 1:1 + E], comb))
            dve.wait_ge(cnt_ps, 1)
            slot = rt[:, 3, :, :]
            link(v.scalar_tensor_tensor(slot, ps[:, 1, 0:TB * E].rearrange("p (t e) -> p t e", t=TB), 1.0,
                                        sel[:, :, :], ALU.add, ALU.mult))
            link(v.tensor_scalar(slot, slot, -1.0, None, ALU.add))
            link(v.tensor_copy(posit[:, :, 1:1 + E], slot))
            for t in range(TB):
                last = v.tensor_scalar(Pm[:, t, :], iota, posit[:, t, 1:2], None, ALU.is_equal)
            last.then_inc(p_ready, 1)
            lo_to(C_MOE + 3)
            p_lo(2, 2)

            def tokens_lo(half, bank=7):
                last = v.tensor_tensor(xel[:, 4 * half:4 * half + 4, :],
                                       ps[:, bank, :].rearrange("p (a n) -> p a n", n=P),
                                       xeh[:, 4 * half:4 * half + 4, :].bitcast(F32), ALU.subtract)
                last.then_inc(m_ev, 1)

            full, nth = rt[:, 4, 0, :], rt[:, 4, 1, :]
            link(v.tensor_scalar(full, ps[:, 1, TB * E:(TB + 1) * E], float(P), None, ALU.is_gt))
            link(v.tensor_tensor(cmpa[:, 0, :, :], full.unsqueeze(1).broadcast_to([P, E, E]), lower8, ALU.mult))
            link(v.tensor_reduce(nth, cmpa[:, 0, :, :], AX.X, ALU.add))
            link(v.tensor_reduce(meta[:, 0:1], full, AX.X, ALU.add))
            pick, part = cmpa[:, 1, 0:3, :], cmpb[:, :, 0:3, :]
            over_p, over_c = posit[:, :, 1 + E:4 + E], combo[:, :, 1 + E:4 + E]

            def by_token(a):
                return a.unsqueeze(1).broadcast_to([P, TB, 3, E])

            def by_item(a):
                return a.unsqueeze(2).broadcast_to([P, TB, 3, E])

            link(v.tensor_tensor(pick, nth.unsqueeze(1).broadcast_to([P, 3, E]),
                                 iota8[:, 0:3].unsqueeze(2).broadcast_to([P, 3, E]), ALU.is_equal))
            link(v.tensor_tensor(pick, pick, full.unsqueeze(1).broadcast_to([P, 3, E]), ALU.mult))
            link(v.tensor_tensor(part, by_item(slot), by_token(pick), ALU.mult))
            link(v.tensor_reduce(over_p, part, AX.X, ALU.add))
            link(v.tensor_scalar(over_p, over_p, -float(P), None, ALU.add))
            dve.wait_ge(xeh_done, 1)
            tokens_lo(0)
            link(v.tensor_tensor(part, by_item(comb), by_token(pick), ALU.mult))
            link(v.tensor_reduce(over_c, part, AX.X, ALU.add))
            link(v.tensor_tensor(pick, pick, iota8.unsqueeze(1).broadcast_to([P, 3, E]), ALU.mult))
            link(v.tensor_reduce(meta[:, 1:4], pick, AX.X, ALU.add))
            v.tensor_copy(metai[:, :], meta[:, :]).then_inc(meta_done, 1)
            dve.wait_ge(xeh_done, 2)
            tokens_lo(1, 6)
            dve.wait_ge(meta_done, 1)
            over = v.value_load(metai[0:1, 0:1], min_val=0, max_val=3)

            def add_scatter(k, item, bank=7):
                t, n = divmod(k, 2)
                to = X[:, t, BANK * n:BANK * (n + 1)]
                return v.scalar_tensor_tensor(to, ps[:, bank, :], combo[:, t, bass.ds(item, 1)], to, ALU.mult, ALU.add)

            with dve.Fori(0, over + E) as i:
                c0 = v.snap(i * EC)
                i7 = v.snap(i * 7)

                def hidden_lo(j):
                    dve.wait_ge(hth_done, i7 + (j + 1))
                    v.tensor_tensor(htl[:, :, :], ps[:, 4, :].rearrange("p (a n) -> p a n", n=P),
                                    hth[:, :, :].bitcast(F32), ALU.subtract).then_inc(ht_done, 1)

                def gathered_lo(half):
                    dve.wait_ge(xeh_done, i * 2 + (2 + half + 1))
                    tokens_lo(half)

                for c in range(EC):
                    if c == EC - 3:
                        hidden_lo(NJ - 1)
                        gathered_lo(1)
                    split_lo(C_MOE + c + 3, shift=c0)
                    if c in (1, 3, 5, 7):
                        dve.wait_ge(m_ps, i7 + (2 + c // 2 + 1))
                        add_scatter(c // 2, i).then_inc(m_ev, 1)
                    if c == 3 or (c > 3 and c % 6 == 1):
                        j = 0 if c == 3 else c // 6
                        dve.wait_ge(msg_done, i7 + (j + 1))
                        v.tensor_tensor(hm[:, j % 2, :], ps[:, 2 * (j % 2) + 1, :], msg[:, :], ALU.mult)\
                            .then_inc(hm_done, 1)
                    if c == 9:
                        dve.wait_ge(m_ps, i7 + (2 + 4 + 1))
                        v.tensor_copy(PmT[:, :], ps[:, 7, 0:S]).then_inc(m_ev, 1)
                        for t in range(TB):
                            last = v.tensor_scalar(Pm[:, t, :], iota, posit[:, t, bass.ds(i + 2, 1)], None, ALU.is_equal)
                        last.then_inc(p_ready, 1)
                    if c % 6 == 5 and c // 6 < NJ - 1:
                        hidden_lo(c // 6)
                    if c == 6 * NJ - 5:
                        gathered_lo(0)
            n_item = v.snap(over + E)
            m0 = v.snap(n_item * 7)
            for k in range(4):
                dve.wait_ge(m_ps, m0 + (2 + k + 1))
                add_scatter(k, n_item, 7 - k).then_inc(fin_scatter, 1)
            c1 = v.snap(n_item * EC)
            norm_rows(N_PLE1, xn_done, 6)
            xT_lo(N_PLE1)
            split_lo(C_MOE + 3, shift=c1)
            split_lo(C_MOE + 4, shift=c1)
            embed(2)
            norm_rows(N_FIN, fin_done, 7)

        @block.tensor
        def _(pe):
            mm = nc.tensor.matmul

            def mm3(to, sh, sl, mh_, ml_, start, stop):
                mm(to, sh, mh_, start=start, stop=False)
                mm(to, sh, ml_, start=False, stop=False)
                return mm(to, sl, mh_, start=False, stop=stop)

            def arrive(n, k, shift=0):
                pe.wait_ge(lo_done, shift + (n + 1))
                return chunk_view(whi, n, k), chunk_view(wlo, n, k)

            def keep_warm(bank, count):
                for _ in range(count):
                    mm(ps[:, bank, 0:P], ident, ident, start=True, stop=True)

            def norm_T(n, idle=0):
                keep_warm(7, idle)
                for t in range(TB):
                    pe.wait_ge(xn_done, 2 * n + t + 1)
                    for k in range(KD):
                        last = nc.tensor.transpose(ps[:, 4 + 2 * t + k // 4, P * (k % 4):P * (k % 4) + P],
                                                   xn[:, t, P * k:P * k + P], ident)
                    last.then_inc(xT_ps, 1)

            def transposed_product(n, m, to):
                wh, wl = chunk_view(whi, n, KD), chunk_view(wlo, n, KD)
                cs = slice(P * m, P * m + P)
                for k in range(KD):
                    a, z = k == 0, k == KD - 1
                    mm(to, wh[:, k, cs], xTh[:, k, :], start=a, stop=False)
                    mm(to, wh[:, k, cs], xTl[:, k, :], start=False, stop=False)
                    last = mm(to, wl[:, k, cs], xTh[:, k, :], start=False, stop=z)
                return last

            def rows_product(n, k0, bank0, sh, sl, first, last_k, shift=0, ready=None):
                wh, wl = arrive(n, 2, shift)
                for t in range(TB):
                    if ready:
                        pe.wait_ge(ready[0], ready[1] + t)
                    ts = slice(P * t, P * t + P)
                    for k in range(2):
                        for half in range(2):
                            cs = slice(BANK * half, BANK * half + BANK)
                            last = mm3(ps[:, bank0 + 2 * t + half, :], sh[:, k0 + k, ts], sl[:, k0 + k, ts],
                                       wh[:, k, cs], wl[:, k, cs], first and k == 0, last_k and k == 1)
                    if last_k and t == 0:
                        last.then_inc(rows_ps, 1)
                return last

            pe.wait_ge(sq_in, 16)
            norm_T(N_MIX0)
            pe.wait_ge(xT_done, 2)

            def w_in(n):
                pe.wait_ge(lo_done, n + 1)
                for m in range(2):
                    blk = 2 * n + m
                    if 4 <= blk < 12:
                        pe.wait_ge(xr_done, blk - 3)
                    elif blk >= 12:
                        pe.wait_ge(gelu_done, blk - 11)
                    last = transposed_product(n, m, ps[:, blk % 4, 0:S])
                    last.then_inc(pe_used if m else in_ps, 1)

            def gate_products(half):
                pe.wait_ge(bd_in, 64)
                for b in range(4 * half, 4 * half + 4):
                    pe.wait_ge(conv_done, b + 1)
                    if half:
                        pe.wait_ge(ri_ev, 2 * (b - 4) + 2)
                    for w in range(2):
                        last = mm(ps[:, 4 + b % 4, S * w:S * w + S], bd[:, w, b, :], xc[:, b, :], start=True, stop=True)
                    last.then_inc(ri_ps, 1)

            w_in(0)
            pe.wait_ge(par_in, 16 * 7)
            nc.tensor.transpose(ps[:, 4, 0:96], par_rows[:, :], ident[0:96, 0:96]).then_inc(setup_ps, 1)
            w_in(1)
            w_in(2)
            pe.wait_ge(prm_done, 1)
            gate_products(0)
            w_in(3)
            w_in(4)
            gate_products(1)
            for n in range(5, 8):
                w_in(n)
            pe.wait_ge(ri_ev, 2 * KD)
            pe.wait_ge(relb_in, 16)
            pe.wait_ge(relb_set, 1)
            pe.wait_ge(hot_in, 16)
            mm(ps[0:H, 4, :], relb[:, :], hotv[:, 0, :], start=True, stop=True).then_inc(setup_ps, 1)
            for b in range(TB):
                for c in range(NC):
                    at_ = P * b - CS * c - (CB - 1) + 256
                    o = (b * NC + c) * H
                    last = mm(ps[:, 5, o:o + H], hotv[:, 1, at_:at_ + P], relb[:, :], start=True, stop=True)
            last.then_inc(setup_ps, 1)
            pe.wait_ge(gelu_done, KD)
            for n in range(4):
                pe.wait_ge(yl_done, n // 2 + 1)
                rows_product(C_OUT + n, 2 * n, 0, xTh, xTl, n == 0, n == 3).then_inc(pe_used, 1)

            pe.wait_ge(setup_ev, 1)
            norm_T(N_FFN0, 12)
            pe.wait_ge(xT_done, 2 * N_FFN0 + 2)

            def down(b, n):
                pe.wait_ge(fhl_done, b + 1)
                rows_product(n, 0, 0, fhh[:, b % 2], fhl[:, b % 2], b == 0, b == NFB - 1).then_inc(pe_used, 1)

            n = C_FFN
            for b in range(NFB):
                if b >= 2:
                    pe.wait_ge(fh_done, b - 1)
                for part in range(2):
                    pe.wait_ge(lo_done, n + 1)
                    for m in range(2):
                        last = transposed_product(n, m, ps[:, 4 + 2 * (b % 2) + m, S * part:S * part + S])
                    last.then_inc(pe_used, 1)
                    n += 1
                if b:
                    down(b - 1, n)
                    n += 1

            def p_T(k, bank):
                pe.wait_ge(p_in, 16 * k)
                for kk in range(2):
                    for t in range(TB):
                        last = nc.tensor.transpose(ps[:, bank, S * kk + P * t:S * kk + P * t + P],
                                                   pn[:, t, P * kk:P * kk + P], ident)
                last.then_inc(pT_ps, 1)

            p_T(1, 4)
            down(NFB - 1, n)
            pe.wait_ge(x_upd, U_PLE0)
            pe.wait_ge(pTl_done, 1)
            rows_product(C_PP0, 0, 0, pTh, pTl, True, True).then_inc(pe_used, 1)
            norm_T(N_PLE0)
            for n in range(4):
                rows_product(C_PG0 + n, 2 * n, 4, xTh, xTl, n == 0, n == 3,
                             ready=None if n else (xT_done, 2 * N_PLE0 + 1)).then_inc(pe_used, 1)
            pe.wait_ge(psg_done, 1)
            keep_warm(4, 12)
            norm_T(N_KV)
            pe.wait_ge(xT_done, 2 * N_KV + 2)

            def narrow_product(n, to):
                wh, wl = arrive(n, KD)
                for k in range(KD):
                    a, z = k == 0, k == KD - 1
                    mm(to, wh[:, k, :], xTh[:, k, :], start=a, stop=False)
                    mm(to, wh[:, k, :], xTl[:, k, :], start=False, stop=False)
                    last = mm(to, wl[:, k, :], xTh[:, k, :], start=False, stop=z)
                return last

            def value_rows(n, bank):
                wh, wl = chunk_view(whi, n, KD), chunk_view(wlo, n, KD)
                for t in range(TB):
                    for k in range(KD):
                        ts = slice(P * t, P * t + P)
                        last = mm3(ps[:, bank, P * t:P * t + P], xTh[:, k, ts], xTl[:, k, ts],
                                   wh[:, k, P:2 * P], wl[:, k, P:2 * P], k == 0, k == KD - 1)
                return last

            pe.wait_ge(lo_done, C_KV + 1)
            transposed_product(C_KV, 0, ps[:, 0, 0:S])
            transposed_product(C_KV, 1, ps[:, 1, 0:S]).then_inc(pe_used, 1)
            pe.wait_ge(lo_done, C_KV + 2)
            transposed_product(C_KV + 1, 0, ps[:, 2, 0:S])
            value_rows(C_KV + 1, 3).then_inc(pe_used, 1)
            pe.wait_ge(lo_done, C_KV + 3)
            transposed_product(C_KV + 2, 0, ps[:, 6, 0:S])
            value_rows(C_KV + 2, 7).then_inc(pe_used, 1)
            pe.wait_ge(ct_ev, 8)
            pe.wait_ge(ml_done, 1)

            def compress(w):
                for part in range(2):
                    wh, wl = arrive(C_W1 + 2 * w + part, 8)
                    for l in range(8):
                        last = mm3(ps[0:G * NC, w, 0:HID], mh[:, w, 8 * part + l, :], ml[:, w, 8 * part + l, :],
                                   wh[:, l, :], wl[:, l, :], part == 0 and l == 0, part == 1 and l == 7)
                    last.then_inc(pe_used, 1)

            def hidden_units():
                pe.wait_ge(hidr_done, 2)
                for w in range(2):
                    for k in range(2):
                        last = nc.tensor.transpose(ps[:, 2, 64 * w + 32 * k:64 * w + 32 * k + G * NC],
                                                   hidr[:, w, P * k:P * k + P], ident[0:G * NC, 0:G * NC])
                last.then_inc(hid_ps, 1)

            def compressed():
                pe.wait_ge(hid_done, 1)
                pe.wait_ge(w2_in, 32)
                for half in range(2):
                    for k in range(2):
                        last = mm(ps[64 * half:64 * half + 64, 0, 0:G * NC], w2s[:, 0, k, :], hid[:, 0, k, :],
                                  start=k == 0, stop=k == 1)
                last.then_inc(w2_ps, 1)
                for g in range(G):
                    for k in range(2):
                        last = mm(ps[0:NC, 1, DH * g:DH * g + DH], hid[:, 1, k, NC * g:NC * g + NC], w2s[:, 1, k, :],
                                  start=k == 0, stop=k == 1)
                last.then_inc(w2_ps, 1)

            compress(0)
            pe.wait_ge(kd_done, 10)
            norm_T(N_MIX1)
            compress(1)
            pe.wait_ge(xT_done, 2 * N_MIX1 + 2)
            for n in range(4):
                pe.wait_ge(lo_done, C_Q + n + 1)
                for m in range(2):
                    blk = 2 * n + m
                    if blk >= 4:
                        pe.wait_ge(q_ev, blk - 3)
                    transposed_product(C_Q + n, m, ps[:, 4 + blk % 4, 0:S]).then_inc(pe_used if m else q_ps, 1)
                if n == 0:
                    hidden_units()
                if n == 1:
                    compressed()
            def compressed_scores(b):
                for h in range(H):
                    hp, par, g = h // 2, h % 2, h // 8
                    hs = slice(64 * par, 64 * par + 64)
                    last = mm(ps[:, 2 * b + par, NC * hp:NC * hp + NC], qT[hs, hp, P * b:P * b + P],
                              kcd[hs, NC * g:NC * g + NC], start=True, stop=True)
                last.then_inc(sc_ps, 1)

            def compressed_probs(b):
                pe.wait_ge(ec_done, b + 1)
                for a in range(4):
                    last = nc.tensor.transpose(ps[:, 4 + b, P * a:P * a + P],
                                               ec[:, 4 * a:4 * a + 4, :].rearrange("p a c -> p (a c)"), ident)
                last.then_inc(ecT_ps, 1)

            def compressed_sums(b, bank):
                pe.wait_ge(ecT_done, b + 1)
                for a in range(4):
                    o = S * (a % 2)
                    last = mm(ps[:, bank + a // 2, o:o + S], ecT[:, a, :], vcb[:, a // 2, :], start=True, stop=True)
                last.then_inc(oc_ps, 1)

            pe.wait_ge(kcd_done, 1)
            pe.wait_ge(vcb_done, 8)
            pe.wait_ge(q_ev, KD)
            narrow_product(C_QG, ps[0:3 * H, 5, 0:S]).then_inc(pe_used, 1)
            compressed_scores(0)
            pe.wait_ge(gtT_done, 1)
            for t in range(TB):
                last = nc.tensor.transpose(ps[:, 5, 48 * t:48 * t + 48], gtT[:, P * t:P * t + P],
                                           ident[0:3 * H, 0:3 * H])
            last.then_inc(gt_ps, 1)
            compressed_scores(1)
            compressed_probs(0)
            compressed_sums(0, 6)
            pe.wait_ge(gt_done, 1)
            compressed_probs(1)

            def scores(n):
                b, h = divmod(n, H)
                if n >= 2:
                    pe.wait_ge(S_done, n - 1)
                if n == 0:
                    pe.wait_ge(ql_done, 4)
                ts = slice(P * b, P * b + P)
                for br in range(2):
                    to = ps[:, n % 2, S * br:S * br + S]
                    mm(to, qs[h % 2][:, h // 2, ts], kdh[:, br, h // 8, :], start=True, stop=False)
                    last = mm(to, qs[h % 2][:, h // 2, ts], kdl[:, br, h // 8, :], start=False, stop=True)
                last.then_inc(S_ps, 1)

            def weighted(n):
                b, h = divmod(n, H)
                pe.wait_ge(PT_done, n + 1)
                if n == H:
                    pe.wait_ge(pv_ev, 2)
                for br in range(2):
                    for k in range(b + 1):
                        o = P * ((b + 1) * br + k)
                        last = mm(ps[:, 4 + 2 * br + h // 8, DH * (h % 8):DH * (h % 8) + DH], PTs[:, n % 2, o:o + P],
                                  vn[:, br, P * k + DH * (h // 8):P * k + DH * (h // 8) + DH],
                                  start=k == 0, stop=k == b)
                last.then_inc(pv_ps, 1)

            scores(0)
            scores(1)
            pe.wait_ge(sc_done, 2)
            for n in range(TB * H):
                b = n // H
                pe.wait_ge(P_done, n + 1)
                if n >= 2:
                    pe.wait_ge(PT_done, n - 1)
                for br in range(2):
                    for k in range(b + 1):
                        o = P * ((b + 1) * br + k)
                        last = nc.tensor.transpose(ps[:, 2 + n % 2, o:o + P], Psb[:, n % 2, br, P * k:P * k + P], ident)
                last.then_inc(PT_ps, 1)
                if n + 2 < TB * H:
                    scores(n + 2)
                if n == 0:
                    compressed_sums(1, 4)
                    pe.wait_ge(oc_ev, 4)
                if n:
                    weighted(n - 1)
            weighted(TB * H - 1)
            pe.wait_ge(PT_done, TB * H)
            pe.wait_ge(S_done, TB * H)
            for t in range(TB):
                for k in range(KD):
                    if k % 4 == 0:
                        pe.wait_ge(o_done, 4 * t + 2 + k // 2)
                    last = nc.tensor.transpose(ps[:, 2 * t + k // 4, P * (k % 4):P * (k % 4) + P],
                                               oac[:, t, P * k:P * k + P], ident)
                last.then_inc(oT_ps, 1)
            pe.wait_ge(lo_half, 2)
            for n in range(4):
                rows_product(C_WO + n, 2 * n, 0, xTh, xTl, n == 0, n == 3,
                             ready=None if n else (oT_done, 1)).then_inc(pe_used, 1)
            norm_T(N_FFN1, 12)
            pe.wait_ge(xT_done, 2 * N_FFN1 + 2)
            narrow_product(C_RT, ps[0:E, 0, 0:S]).then_inc(pe_used, 1)
            pe.wait_ge(lgT_done, 1)
            for t in range(TB):
                last = nc.tensor.transpose(ps[:, 0, E * t:E * t + E], lgT[:, P * t:P * t + P], ident[0:E, 0:E])
            last.then_inc(lg_ps, 1)
            p_T(2, 2)
            pe.wait_ge(sel_done, 1)
            pe.wait_ge(relb_set, 2)
            mm(ps[:, 1, 0:E], before, sel[:, 0, :], start=True, stop=True)
            mm(ps[:, 1, E:2 * E], ones[:, :], sel[:, 0, :], start=True, stop=False)
            mm(ps[:, 1, E:2 * E], before, sel[:, 1, :], start=False, stop=True)
            mm(ps[:, 1, 2 * E:3 * E], ones[:, :], sel[:, 0, :], start=True, stop=False)
            mm(ps[:, 1, 2 * E:3 * E], ones[:, :], sel[:, 1, :], start=False, stop=True).then_inc(cnt_ps, 1)

            def gather(half, bank=7):
                for c in range(4):
                    for t in range(TB):
                        o = P * (4 * half + c)
                        last = mm(ps[:, bank, P * c:P * c + P], xn[:, t, o:o + P], Pm[:, t, :], start=t == 0, stop=t == 1)
                last.then_inc(m_ps, 1)

            def scatter(k, bank=7):
                t, n = divmod(k, 2)
                mm(ps[:, bank, :], PmT[:, P * t:P * t + P], osb[:, BANK * n:BANK * (n + 1)], start=True, stop=True)\
                    .then_inc(m_ps, 1)

            pe.wait_ge(p_ready, 1)
            gather(0)
            gather(1, 6)
            pe.wait_ge(pTl_done, 2)
            pe.wait_ge(meta_done, 1)
            over = nc.tensor.value_load(metai[0:1, 0:1], min_val=0, max_val=3)
            with pe.Fori(0, over + E) as i:
                c0 = nc.tensor.snap(i * EC)
                i7 = nc.tensor.snap(i * 7)

                def gate_up(c, j, half):
                    for part in range(2):
                        wh, wl = arrive(C_MOE + c + part, 4, c0)
                        for k in range(4):
                            kk = 4 * half + k
                            last = mm3(ps[:, 2 * (j % 2) + part, :], xeh[:, kk, :], xel[:, kk, :], wh[:, k, :],
                                       wl[:, k, :], kk == 0, kk == KD - 1)
                        last.then_inc(pe_used, 1)

                def hidden_T(j):
                    pe.wait_ge(hm_done, i7 + (HM0 + j + 1))
                    pe.wait_ge(ht_done, i7 + (HT0 + j))
                    for f in range(4):
                        last = nc.tensor.transpose(ps[:, 4, P * f:P * f + P], hm[:, j % 2, P * f:P * f + P], ident)
                    last.then_inc(t_ps, 1)

                def down_rows(c, j):
                    pe.wait_ge(ht_done, i7 + (HT0 + j + 1))
                    if j == 0:
                        pe.wait_ge(osb_done, i + OS0)
                    for part in range(2):
                        wh, wl = arrive(C_MOE + c + part, 2, c0)
                        for k in range(2):
                            f = 2 * part + k
                            for n in range(2):
                                cs = slice(BANK * n, BANK * n + BANK)
                                last = mm3(ps[:, 5 + n, :], hth[:, f, :], htl[:, f, :], wh[:, k, cs], wl[:, k, cs],
                                           j == 0 and f == 0, j == NJ - 1 and f == 3)
                        last.then_inc(pe_used, 1)

                pe.wait_ge(m_ev, i7 + 2)
                c = 0
                for j in range(NJ):
                    pe.wait_ge(hm_done, i7 + (HM0 + j - 1))
                    gate_up(c, j, 0)
                    c += 2
                    if j < 2:
                        if j == 0:
                            pe.wait_ge(osb_done, i + OS0)
                        pe.wait_ge(m_ev, i7 + (2 + 2 * j))
                        scatter(2 * j)
                    if j:
                        hidden_T(j - 1)
                    if j == NJ - 1:
                        pe.wait_ge(p_ready, i + 2)
                        pe.wait_ge(m_ev, i7 + (2 + 5))
                        gather(0)
                    gate_up(c, j, 1)
                    c += 2
                    if j < 2:
                        pe.wait_ge(m_ev, i7 + (2 + 2 * j + 1))
                        scatter(2 * j + 1)
                    if j:
                        down_rows(c, j - 1)
                        c += 2
                    if j == 1:
                        pe.wait_ge(m_ev, i7 + (2 + 4))
                        for t in range(TB):
                            last = nc.tensor.transpose(ps[:, 7, P * t:P * t + P], Pm[:, t, :], ident)
                        last.then_inc(m_ps, 1)
                hidden_T(NJ - 1)
                pe.wait_ge(m_ev, i7 + (2 + 6))
                gather(1)
                down_rows(c, NJ - 1)
            n_item = nc.tensor.snap(over + E)
            c1 = nc.tensor.snap(n_item * EC)
            m0 = nc.tensor.snap(n_item * 7)
            pe.wait_ge(osb_done, n_item + OS0)
            pe.wait_ge(m_ev, m0 + 2)
            for k in range(4):
                scatter(k, 7 - k)
            pe.wait_ge(hm_done, m0 + HM0)

            rows_product(C_MOE, 0, 0, pTh, pTl, True, True, shift=c1).then_inc(pe_used, 1)
            pe.wait_ge(fin_scatter, 4)
            norm_T(N_PLE1)
            for n in range(4):
                rows_product(C_MOE + 1 + n, 2 * n, 4, xTh, xTl, n == 0, n == 3, shift=c1,
                             ready=None if n else (xT_done, 2 * N_PLE1 + 1)).then_inc(pe_used, 1)


_INS = ['x', 'p', 'g_mix', 'g_ffn', 'g_ple', 'g_final', 'rg_w_in', 'rg_conv_w', 'rg_conv_b', 'rg_w_a', 'rg_b_a',
        'rg_w_x', 'rg_b_x', 'rg_lambda', 'rg_w_out', 'kv_norm', 'w_kv', 'cmp_pos_k', 'cmp_pos_v', 'cmp_k_w1',
        'cmp_k_w2', 'cmp_v_w1', 'cmp_v_w2', 'rel_bias', 'nsa_w_q', 'nsa_w_o', 'ffn_w_gu', 'ffn_w_down',
        'moe_w_router', 'moe_w_gu', 'moe_w_down', 'ple_w_proj', 'ple_w_gate']


def kernel(**inputs):
    import concourse.bacc as _bacc
    from concourse.bass_utils import run_bass_kernel_spmd as _run

    nc = _bacc.Bacc("TRN2", target_bir_lowering=False, num_devices=1)
    square, hot = shape_constants()
    arrays, args = {}, []
    for name in _INS + ['square', 'hot']:
        a = {'square': square, 'hot': hot}.get(name)
        a = np.ascontiguousarray(inputs[name] if a is None else a)
        arrays[f"in_{name}_dram"] = a
        args.append(nc.dram_tensor(f"in_{name}_dram", a.shape, mybir.dt.from_np(a.dtype), kind="ExternalInput").ap())
    res = nc.dram_tensor("out_dram", (1, S, D), F32, kind="ExternalOutput").ap()
    trunk(nc, *args, res)
    r = _run(nc, [arrays], core_ids=[0])
    return r.results[0]["out_dram"]
```
